# Optimizing a Trainium2 kernel written in Bass

```python
import jax, jax.numpy as jnp
from jax import lax
import numpy as np

D_MODEL = 1024
BATCH = 1
SEQ = 256
DEPTH = 2

GRID_W = 64
CTX_LEN = 256
N_EVEN = (DEPTH + 1) // 2
N_ODD = DEPTH // 2
N_MOD = 9
D_FF = 2816
EPS = 1e-6
CONV_DIM = D_MODEL // 2
CONV_WIDTH = 31
CONV_PAD = (CONV_WIDTH - 1) // 2
HEAD_DIM = 64
ATT_HEADS = 8
ATT_KV_HEADS = 2
ATT_GROUP = ATT_HEADS // ATT_KV_HEADS
ATT_DIM = ATT_HEADS * HEAD_DIM
KV_DIM = ATT_KV_HEADS * HEAD_DIM
WINDOW = 128
BLOCK = 128
ROPE_BASE = 10000.0
ROPE_FREQS = HEAD_DIM // 4
Q_OFF = 2 * CONV_DIM
K_OFF = Q_OFF + ATT_DIM
V_OFF = K_OFF + KV_DIM
EVEN_IN = V_OFF + KV_DIM
EVEN_MIX = CONV_DIM + ATT_DIM
ML_HEADS = 4
ML_HEAD_DIM = D_MODEL // ML_HEADS
ML_DIM = ML_HEADS * ML_HEAD_DIM
ML_CHUNK = 128
ODD_IN = 4 * ML_DIM + 4 * ML_HEADS
FORGET_BIAS = 3.0

kernel_name = "hybrid_conv_swa_mlstm_dit_prefix"

def rmsnorm(x, g):
    xf = x.astype(jnp.float32)
    y = xf * lax.rsqrt(jnp.mean(xf * xf, axis=-1, keepdims=True) + EPS)
    return (y * g.astype(jnp.float32)).astype(x.dtype)

def layernorm(x, g, b):
    xf = x.astype(jnp.float32)
    mu = jnp.mean(xf, axis=-1, keepdims=True)
    var = jnp.mean(jnp.square(xf - mu), axis=-1, keepdims=True)
    return ((xf - mu) * lax.rsqrt(var + EPS) * g.astype(jnp.float32) + b.astype(jnp.float32)).astype(x.dtype)

def ada_params(cond, w, b):
    m = (jax.nn.silu(cond) @ w + b)[..., None, :]
    return jnp.split(m, N_MOD, axis=-1)

def modulate(x, shift, scale):
    return x * (1 + scale) + shift

def ffn_half(x, mods, g, w_gu, w_d):
    shift, scale, gate = mods
    h = modulate(rmsnorm(x, g), shift, scale) @ w_gu
    hg, hu = jnp.split(h, 2, axis=-1)
    return x + 0.5 * gate * ((jax.nn.silu(hg) * hu) @ w_d)

def axial_rope_tables(n):
    rows = n // GRID_W
    row = jnp.repeat(jnp.arange(rows, dtype=jnp.float32), GRID_W)
    col = jnp.tile(jnp.arange(GRID_W, dtype=jnp.float32), rows)
    inv = ROPE_BASE ** (-jnp.arange(ROPE_FREQS, dtype=jnp.float32) / ROPE_FREQS)
    ang = jnp.concatenate([row[:, None] * inv, col[:, None] * inv], axis=-1)
    return jnp.cos(ang), jnp.sin(ang)

def apply_rope(x, cos, sin):
    n = x.shape[1]
    xr = x.astype(jnp.float32).reshape(x.shape[:-1] + (2, 2, ROPE_FREQS))
    x1, x2 = xr[..., 0, :], xr[..., 1, :]
    c = cos.reshape(n, 1, 2, ROPE_FREQS)
    s = sin.reshape(n, 1, 2, ROPE_FREQS)
    out = jnp.stack([x1 * c - x2 * s, x2 * c + x1 * s], axis=-2)
    return out.reshape(x.shape).astype(x.dtype)

def conv_module(val, gate, w_dw, b_dw, ln_g, ln_b):
    u = val * jax.nn.sigmoid(gate)
    u = lax.conv_general_dilated(u, w_dw[:, None, :], window_strides=(1,), padding=[(CONV_PAD, CONV_PAD)],
                                 dimension_numbers=("NWC", "WIO", "NWC"), feature_group_count=CONV_DIM) + b_dw
    return jax.nn.silu(layernorm(u, ln_g, ln_b))

def banded(t, nb):
    tb = t.reshape(t.shape[0], nb, BLOCK, ATT_KV_HEADS, HEAD_DIM)
    tp = jnp.pad(tb, ((0, 0), (1, 1), (0, 0), (0, 0), (0, 0)))
    return jnp.concatenate([tp[:, :-2], tp[:, 1:-1], tp[:, 2:]], axis=2)

def band_mask(nb):
    r = jnp.arange(BLOCK)[:, None]
    j = jnp.arange(3 * BLOCK)[None, :]
    rel = j - BLOCK - r
    kpos = (jnp.arange(nb)[:, None, None] - 1) * BLOCK + j[None]
    return (jnp.abs(rel) <= WINDOW)[None] & (kpos >= 0) & (kpos < nb * BLOCK)

def sink_logits(sink, shape):
    s = sink.astype(jnp.float32).reshape((1, ATT_KV_HEADS, ATT_GROUP) + (1,) * (len(shape) - 3))
    return jnp.broadcast_to(s, shape[:-1] + (1,))

def window_attn_latent(q, k, v, kc, vc, sink):
    B, S = q.shape[:2]
    nb = S // BLOCK
    nk = 3 * BLOCK
    ncx = kc.shape[1]
    scale = HEAD_DIM ** -0.5
    qb = q.reshape(B, nb, BLOCK, ATT_KV_HEADS, ATT_GROUP, HEAD_DIM)
    kb, vb = banded(k, nb), banded(v, nb)
    s_band = jnp.einsum("bnqkgd,bnjkd->bkgnqj", qb, kb).astype(jnp.float32) * scale
    s_band = jnp.where(band_mask(nb), s_band, -jnp.inf)
    s_ctx = jnp.einsum("bnqkgd,bckd->bkgnqc", qb, kc).astype(jnp.float32) * scale
    p = jax.nn.softmax(jnp.concatenate([s_band, s_ctx, sink_logits(sink, s_band.shape)], axis=-1), axis=-1)
    o = (jnp.einsum("bkgnqj,bnjkd->bnqkgd", p[..., :nk].astype(v.dtype), vb)
         + jnp.einsum("bkgnqc,bckd->bnqkgd", p[..., nk:nk + ncx].astype(v.dtype), vc))
    return o.reshape(B, S, ATT_DIM)

def attn_context(qc, kc, vc, sink):
    B, C = qc.shape[:2]
    qg = qc.reshape(B, C, ATT_KV_HEADS, ATT_GROUP, HEAD_DIM)
    s = jnp.einsum("bqkgd,bckd->bkgqc", qg, kc).astype(jnp.float32) * HEAD_DIM ** -0.5
    p = jax.nn.softmax(jnp.concatenate([s, sink_logits(sink, s.shape)], axis=-1), axis=-1)
    o = jnp.einsum("bkgqc,bckd->bqkgd", p[..., :C].astype(vc.dtype), vc)
    return o.reshape(B, C, ATT_DIM)

def even_mixer(hl, hc, w_in, conv_w, conv_b, ln_g, ln_b, sink, w_out, cos, sin, with_ctx_out):
    B, S, _ = hl.shape
    C = hc.shape[1]
    pl = hl @ w_in
    a_l = conv_module(pl[..., :CONV_DIM], pl[..., CONV_DIM:Q_OFF], conv_w, conv_b, ln_g, ln_b)
    q = apply_rope(pl[..., Q_OFF:K_OFF].reshape(B, S, ATT_HEADS, HEAD_DIM), cos, sin)
    k = apply_rope(pl[..., K_OFF:V_OFF].reshape(B, S, ATT_KV_HEADS, HEAD_DIM), cos, sin)
    v = pl[..., V_OFF:].reshape(B, S, ATT_KV_HEADS, HEAD_DIM)
    pkv = hc @ w_in[:, K_OFF:]
    kc = pkv[..., :KV_DIM].reshape(B, C, ATT_KV_HEADS, HEAD_DIM)
    vc = pkv[..., KV_DIM:].reshape(B, C, ATT_KV_HEADS, HEAD_DIM)
    att_l = window_attn_latent(q, k, v, kc, vc, sink)
    yl = jnp.concatenate([a_l, att_l], axis=-1) @ w_out
    if not with_ctx_out:
        return yl, None
    pc = hc @ w_in[:, :K_OFF]
    a_c = conv_module(pc[..., :CONV_DIM], pc[..., CONV_DIM:Q_OFF], conv_w, conv_b, ln_g, ln_b)
    att_c = attn_context(pc[..., Q_OFF:].reshape(B, C, ATT_HEADS, HEAD_DIM), kc, vc, sink)
    yc = jnp.concatenate([a_c, att_c], axis=-1) @ w_out
    return yl, yc

def mlstm_zero_state(B):
    f32 = jnp.float32
    return (jnp.zeros((B, ML_HEADS, ML_HEAD_DIM, ML_HEAD_DIM), f32),
            jnp.zeros((B, ML_HEADS, ML_HEAD_DIM), f32),
            jnp.zeros((B, ML_HEADS), f32))

def mlstm_scan(q, k, v, i_pre, f_pre, state, with_out):
    B, n, H, dh = q.shape
    nc = n // ML_CHUNK
    f32 = jnp.float32

    def chunks(t):
        return jnp.moveaxis(t.astype(f32).reshape((B, nc, ML_CHUNK) + t.shape[2:]), 1, 0)

    xs = (chunks(q), chunks(k * dh ** -0.5), chunks(v), chunks(i_pre),
          chunks(jax.nn.log_sigmoid(f_pre.astype(f32))))
    causal = jnp.tril(jnp.ones((ML_CHUNK, ML_CHUNK), bool))[None, :, :, None]

    def step(carry, inp):
        Cm, nv, m = carry
        qc, kc, vc, li, lf = inp
        b = jnp.cumsum(lf, axis=1)
        b_end = b[:, -1]
        w_end = b_end[:, None] - b + li
        m_new = jnp.maximum(b_end + m, jnp.max(w_end, axis=1))
        decay = jnp.exp(b_end + m - m_new)
        wk = jnp.exp(w_end - m_new[:, None])[..., None] * kc
        C_new = decay[..., None, None] * Cm + jnp.einsum("blhv,blhk->bhvk", vc, wk)
        n_new = decay[..., None] * nv + jnp.sum(wk, axis=1)
        if not with_out:
            return (C_new, n_new, m_new), None
        dmat = jnp.where(causal, b[:, :, None] - b[:, None] + li[:, None], -jnp.inf)
        inter = b + m[:, None]
        m_q = jnp.maximum(jnp.max(dmat, axis=2), inter)
        s = jnp.einsum("bqhd,bkhd->bqkh", qc, kc) * jnp.exp(dmat - m_q[:, :, None])
        w_inter = jnp.exp(inter - m_q)
        num = (jnp.einsum("bqkh,bkhd->bqhd", s, vc)
               + w_inter[..., None] * jnp.einsum("bhvk,bqhk->bqhv", Cm, qc))
        den = jnp.sum(s, axis=2) + w_inter * jnp.einsum("bhk,bqhk->bqh", nv, qc)
        h = num / jnp.maximum(jnp.abs(den), jnp.exp(-m_q))[..., None]
        return (C_new, n_new, m_new), h

    state, hs = lax.scan(step, state, xs)
    if with_out:
        hs = jnp.moveaxis(hs, 0, 1).reshape(B, n, H, dh)
    return state, hs

def odd_mixer(hl, hc, w_in, b_gate, norm_g, w_out, with_ctx_out):
    def qkv_gates(h):
        B, n, _ = h.shape
        qkv = (h @ w_in[:, :3 * ML_DIM]).reshape(B, n, 3, ML_HEADS, ML_HEAD_DIM)
        g = (h @ w_in[:, 4 * ML_DIM:] + b_gate).astype(jnp.float32).reshape(B, n, 4, ML_HEADS)
        return qkv[:, :, 0], qkv[:, :, 1], qkv[:, :, 2], g

    def out(h, h_sum):
        B, n, _ = h.shape
        o = jax.nn.sigmoid(h @ w_in[:, 3 * ML_DIM:4 * ML_DIM])
        hn = h_sum * lax.rsqrt(jnp.mean(h_sum * h_sum, axis=-1, keepdims=True) + EPS)
        hn = hn.reshape(B, n, ML_DIM) * norm_g.astype(jnp.float32)
        return (o * hn.astype(h.dtype)) @ w_out

    flip = lambda t: jnp.flip(t, axis=1)
    ql, kl, vl, gl = qkv_gates(hl)
    qc, kc, vc, gc = qkv_gates(hc)
    z = mlstm_zero_state(hl.shape[0])
    st_f, hcf = mlstm_scan(qc, kc, vc, gc[:, :, 0], gc[:, :, 1], z, with_ctx_out)
    st_b, hcb = mlstm_scan(flip(qc), flip(kc), flip(vc), flip(gc[:, :, 2]), flip(gc[:, :, 3]), z, with_ctx_out)
    _, hlf = mlstm_scan(ql, kl, vl, gl[:, :, 0], gl[:, :, 1], st_f, True)
    _, hlb = mlstm_scan(flip(ql), flip(kl), flip(vl), flip(gl[:, :, 2]), flip(gl[:, :, 3]), st_b, True)
    yl = out(hl, hlf + flip(hlb))
    if not with_ctx_out:
        return yl, None
    return yl, out(hc, hcf + flip(hcb))

def setup_inputs(seed: int = 0) -> dict:
    key = jax.random.key(seed)
    ks = iter(jax.random.split(key, 32))
    f32 = jnp.float32
    D = D_MODEL

    def nrm(shape, s):
        return jax.random.normal(next(ks), shape, f32) * s

    def gain(shape):
        return 1.0 + nrm(shape, 0.02)

    gate_offset = jnp.tile(jnp.repeat(jnp.array([0.0, FORGET_BIAS], f32), ML_HEADS), 2)
    return {
        "x": nrm((BATCH, SEQ, D), 1.0),
        "c": nrm((BATCH, D), 1.0),
        "ctx": nrm((BATCH, CTX_LEN, D), 1.0),
        "c_ctx": nrm((D,), 1.0),
        "mod_w": nrm((DEPTH, D, N_MOD * D), 0.5 * D ** -0.5),
        "mod_b": nrm((DEPTH, N_MOD * D), 0.02),
        "ffn1_norm": gain((DEPTH, D)),
        "ffn1_w_gu": nrm((DEPTH, D, 2 * D_FF), D ** -0.5),
        "ffn1_w_d": nrm((DEPTH, D_FF, D), D_FF ** -0.5),
        "mix_norm": gain((DEPTH, D)),
        "ffn2_norm": gain((DEPTH, D)),
        "ffn2_w_gu": nrm((DEPTH, D, 2 * D_FF), D ** -0.5),
        "ffn2_w_d": nrm((DEPTH, D_FF, D), D_FF ** -0.5),
        "ev_w_in": nrm((N_EVEN, D, EVEN_IN), D ** -0.5),
        "ev_conv_w": nrm((N_EVEN, CONV_WIDTH, CONV_DIM), CONV_WIDTH ** -0.5),
        "ev_conv_b": nrm((N_EVEN, CONV_DIM), 0.02),
        "ev_conv_ln_g": gain((N_EVEN, CONV_DIM)),
        "ev_conv_ln_b": nrm((N_EVEN, CONV_DIM), 0.02),
        "ev_sink": nrm((N_EVEN, ATT_HEADS), 0.5),
        "ev_w_out": nrm((N_EVEN, EVEN_MIX, D), EVEN_MIX ** -0.5),
        "od_w_in": nrm((N_ODD, D, ODD_IN), D ** -0.5),
        "od_b_gate": gate_offset[None] + nrm((N_ODD, 4 * ML_HEADS), 0.3),
        "od_norm_g": gain((N_ODD, ML_DIM)),
        "od_w_out": nrm((N_ODD, ML_DIM, D), ML_DIM ** -0.5),
        "final_norm": gain((D,)),
    }

def reference(x, c, ctx, c_ctx, mod_w, mod_b, ffn1_norm, ffn1_w_gu, ffn1_w_d, mix_norm,
              ffn2_norm, ffn2_w_gu, ffn2_w_d, ev_w_in, ev_conv_w, ev_conv_b, ev_conv_ln_g,
              ev_conv_ln_b, ev_sink, ev_w_out, od_w_in, od_b_gate, od_norm_g, od_w_out, final_norm):
    cos, sin = axial_rope_tables(x.shape[1])
    xl, xc = x, ctx
    for l in range(DEPTH):
        last = l == DEPTH - 1
        ml = ada_params(c, mod_w[l], mod_b[l])
        mc = ada_params(c_ctx, mod_w[l], mod_b[l])
        xl = ffn_half(xl, ml[0:3], ffn1_norm[l], ffn1_w_gu[l], ffn1_w_d[l])
        xc = ffn_half(xc, mc[0:3], ffn1_norm[l], ffn1_w_gu[l], ffn1_w_d[l])
        hl = modulate(rmsnorm(xl, mix_norm[l]), ml[3], ml[4])
        hc = modulate(rmsnorm(xc, mix_norm[l]), mc[3], mc[4])
        j = l // 2
        if l % 2 == 0:
            yl, yc = even_mixer(hl, hc, ev_w_in[j], ev_conv_w[j], ev_conv_b[j], ev_conv_ln_g[j],
                                ev_conv_ln_b[j], ev_sink[j], ev_w_out[j], cos, sin, not last)
        else:
            yl, yc = odd_mixer(hl, hc, od_w_in[j], od_b_gate[j], od_norm_g[j], od_w_out[j], not last)
        xl = xl + ml[5] * yl
        xl = ffn_half(xl, ml[6:9], ffn2_norm[l], ffn2_w_gu[l], ffn2_w_d[l])
        if not last:
            xc = xc + mc[5] * yc
            xc = ffn_half(xc, mc[6:9], ffn2_norm[l], ffn2_w_gu[l], ffn2_w_d[l])
    return rmsnorm(xl, final_norm)


_drawn_inputs = setup_inputs


def setup_inputs(seed=0):
    import zlib

    import numpy as np

    out = dict(_drawn_inputs(seed))
    spreads = {}
    factors = {'ffn1_norm': 8.0,
     'mix_norm': 6.194,
     'ffn2_norm': 8.0,
     'ev_conv_b': 29.833,
     'ev_conv_ln_g': 52.407,
     'ev_conv_ln_b': 48.128,
     'ev_sink': 8.0,
     'od_norm_g': 64.0,
     'final_norm': 8.192}
    for name, (base, spread) in spreads.items():
        noise = np.random.default_rng([zlib.crc32(name.encode()), seed]).standard_normal(out[name].shape)
        drawn = base * np.exp(spread * noise) if base else spread * noise
        out[name] = __import__('jax').numpy.asarray(drawn.astype(out[name].dtype))
    for name, factor in factors.items():
        out[name] = (out[name] * factor).astype(out[name].dtype)
    return out
```

```python
from contextlib import ExitStack

import numpy as np

import concourse.bass as bass
from concourse import mybir

P = 128
D = 1024
KT = D // P
LAT = 256
TOK = 2 * LAT
FF = 2816
FT = FF // P
PARTS = (12, 10)
EPS = 1e-6
CONV_W = 31
PAD = (CONV_W - 1) // 2
PADDED = LAT + 2 * PAD
CT = 4
HD = 64
NH_ATT = 8
KEYS = TOK
WINDOW = 128
HM = 4
DH = 256
GRID_W = 64
ROPE_FREQS = 16
NVEC = 9
JOBS = 2 * NVEC
UNIT = 2048
BIG = 1e30
F32 = mybir.dt.float32
F32R = mybir.dt.float32r
ALU = mybir.AluOpType
ACT = mybir.ActivationFunctionType
AX = mybir.AxisListType

COLS = {}
_at = 0
for _name, _n in (("ffn1", 16), ("mix", 16), ("ffn2", 16), ("final", 8), ("conv_b", 4), ("ln_g", 4), ("ln_b", 4),
                  ("norm_g", 8), ("conv_w", CONV_W * CT), ("mod_b", JOBS * KT), ("sink", NH_ATT), ("b_gate", 4 * HM)):
    COLS[_name] = (_at, _n)
    _at += _n
NCOL = _at

MATS = ("ident", "ones", "tri_up", "tri_low", "hide_after", "hide_before", "rot")
NMAT = len(MATS)


def schedule():
    base, size = {}, []

    def add(name, n, elements):
        base[name] = len(size)
        size.extend([elements] * n)

    def ffn(name):
        for part, n in zip("AB", PARTS):
            add(f"{name}up{part}", n, UNIT)
            add(f"{name}down{part}", KT, n * P)

    ffn("f0")
    add("ev_in", 7, UNIT)
    add("ev_out", 4, UNIT)
    ffn("f1")
    ffn("f2")
    add("od_gate", 1, KT * 4 * HM)
    add("od_in", 16, UNIT)
    add("od_out", 4, UNIT)
    ffn("f3")
    return base, size


def build(nc, t, out):
    U, SIZE = schedule()
    NU = len(SIZE)
    with ExitStack() as ctx:
        def sb(name, shape, dt=F32, scope=ctx):
            return scope.enter_context(nc.sbuf_tensor(name, shape, dt))

        def sem(name):
            return ctx.enter_context(nc.semaphore(name))

        xT = sb("xT", [P, KT, TOK])
        hn_hi = sb("hn_hi", [P, KT, TOK], F32R)
        hn_lo = sb("hn_lo", [P, KT, TOK], F32R)
        raw = sb("raw", [P, 2, UNIT])
        w_hi = sb("w_hi", [P, 2, UNIT], F32R)
        w_lo = sb("w_lo", [P, 2, UNIT], F32R)
        gact = sb("gact", [P, 2, TOK])
        prod = sb("prod", [P, 2, TOK])
        t_ring = sb("t_ring", [P, 2, TOK])
        sq = sb("sq", [P, 2, TOK])
        acc = sb("acc", [P, TOK])
        sd = sb("sd", [P, TOK])
        rstd = sb("rstd", [P, TOK])
        mats = sb("mats", [P, NMAT, P])
        cols = sb("cols", [P, NCOL])
        sel = sb("sel", [P, 8])
        shared = sb("shared", [P, 2 * LAT])
        mrow = shared[:, 0:LAT]
        c_in = mrow
        c_act = shared[:, LAT:2 * LAT].rearrange("p (k c) -> p k c", k=KT)
        modT = sb("modT", [P, JOBS, KT, 2])
        mat = {n: mats[:, i, :] for i, n in enumerate(MATS)}
        ident, ones = mat["ident"], mat["ones"]

        with ExitStack() as s:
            a_hi = sb("a_hi", [P, PARTS[0], TOK], F32R, s)
            a_lo = sb("a_lo", [P, PARTS[0], TOK], F32R, s)
            mod_raw = sb("mod_raw", [P, KT, D], F32, s)
        with ExitStack() as s:
            mod_raw1 = sb("mod_raw1", [P, KT, D], F32, s)
        with ExitStack() as s:
            upad = sb("upad", [P, CT, 2, PADDED], F32, s)
            y = sb("y", [P, CT, TOK], F32, s)
            qk = sb("qk", [P, CT + 1, TOK], F32, s)
            v_att = sb("v_att", [P, 4, P], F32, s)
            cos_sin = sb("cos_sin", [P, 2, LAT], F32, s)
            att_mask = sb("att_mask", [P, 2, KEYS], F32, s)
            pT = sb("pT", [P, 2, 4, LAT], F32, s)
            att_cols = sb("att_cols", [P, 6, 32], F32, s)
        with ExitStack() as s:
            k_tok = sb("k_tok", [P, 4, HM, DH], F32, s)
            v_tok = sb("v_tok", [P, 4, HM, DH + 1], F32, s)
            qT = sb("qT", [P, KT, LAT], F32, s)
            kT = sb("kT", [P, KT, LAT], F32, s)
            oT = sb("oT", [P, KT, LAT], F32, s)
            state = sb("state", [P, 2, HM, 2, DH + 1], F32, s)
            decayed = sb("decayed", [P, 2, 2, HM, P], F32, s)
            out_cols = sb("out_cols", [P, 2, 16], F32, s)
            ms_cols = sb("ms_cols", [P, 2, 8], F32, s)
        gates = shared[:].rearrange("p (n d s h) -> p n d s h", d=2, s=4, h=HM)
        GATE = {n: gates[:, i] for i, n in enumerate(
            ("li", "f", "abs", "exp", "ln", "lf", "b", "end", "a", "amax", "cmax", "m", "mm", "mq", "arg", "val"))}

        ps = ctx.enter_context(nc.psum_tensor("ps", [P, 8, TOK], F32))

        unit_in = [sem("unit_in0"), sem("unit_in1")]
        hi_made = sem("hi_made")
        lo_made = sem("lo_made")
        unit_mm = sem("unit_mm")
        unit_evac = sem("unit_evac")
        gate_made = sem("gate_made")
        a_hi_made = sem("a_hi_made")
        a_made = sem("a_made")
        x_in = sem("x_in")
        sq_made = sem("sq_made")
        sq_added = sem("sq_added")
        acc_clear = sem("acc_clear")
        norm_mm = sem("norm_mm")
        ms_made = sem("ms_made")
        sd_made = sem("sd_made")
        rstd_made = sem("rstd_made")
        t_made = sem("t_made")
        hn_hi_made = sem("hn_hi_made")
        hn_made = sem("hn_made")
        par_in = sem("par_in")
        c_made = sem("c_made")
        mod_first = [sem("mod_first0"), sem("mod_first1")]
        mod_in = sem("mod_in")
        mod_mm = sem("mod_mm")
        mod_row = sem("mod_row")
        mod_tr = sem("mod_tr")
        mod_made = sem("mod_made")
        link_v = sem("link_v")
        link_s = sem("link_s")
        ev_in = sem("ev_in")
        tap_done = sem("tap_done")
        pad_clear = sem("pad_clear")
        qk_raw = sem("qk_raw")
        rot_mm = sem("rot_mm")
        roped = sem("roped")
        conv_done = sem("conv_done")
        ln_mm = sem("ln_mm")
        ln_cent = sem("ln_cent")
        ln_sq = sem("ln_sq")
        ln_ms = sem("ln_ms")
        ln_sd = sem("ln_sd")
        ln_t = sem("ln_t")
        ln_hi = sem("ln_hi")
        mix_made = sem("mix_made")
        s_mm = sem("s_mm")
        max_made = sem("max_made")
        exp_made = sem("exp_made")
        p_made = sem("p_made")
        pT_mm = sem("pT_mm")
        pT_made = sem("pT_made")
        pv_mm = sem("pv_mm")
        att_hi = sem("att_hi")
        g_in = sem("g_in")
        ln1p = sem("ln1p")
        lf_made = sem("lf_made")
        cum_mm = sem("cum_mm")
        diag_made = sem("diag_made")
        diag_mm = sem("diag_mm")
        diag_free = sem("diag_free")
        arg_made = sem("arg_made")
        val_made = sem("val_made")
        hid_made = sem("hid_made")
        dec_made = sem("dec_made")
        kT_mm = sem("kT_mm")
        kT_made = sem("kT_made")
        st_mm = sem("st_mm")
        sT_made = sem("sT_made")
        wk_made = sem("wk_made")
        st_up = sem("st_up")
        st_made = sem("st_made")
        out_mm = sem("out_mm")
        out_scaled = sem("out_scaled")
        out_made = sem("out_made")
        h_made = sem("h_made")
        ss_made = sem("ss_made")
        hms_made = sem("hms_made")
        hsd_made = sem("hsd_made")
        hnorm = sem("hnorm")
        hT_mm = sem("hT_mm")
        hz_made = sem("hz_made")
        hz_hi = sem("hz_hi")
        y_made = sem("y_made")
        y_out = [sem("y_out0"), sem("y_out1")]

        FFNS = (("f0", 0, 0, TOK), ("f1", 1, 2, TOK), ("f2", 2, 3, TOK), ("f3", 3, 5, LAT))
        CONV_G = FT
        GBASE = {"f0": 0, "f1": FT + CT, "f2": 2 * FT + CT, "f3": 3 * FT + CT}
        ABASE = {"f0": 0, "f1": FT, "f2": 2 * FT, "f3": 3 * FT}
        OD_G = GBASE["f3"]
        GBASE["f3"] += 4
        W = [TOK] * 5 + [LAT] * 2
        GAIN = [("ffn1", 0), ("mix", 0), ("ffn2", 0), ("ffn1", KT), ("mix", KT), ("ffn2", KT), ("final", 0)]
        JOB_OF = {"f0A": (2, 6), "f0B": (8, 5), "f1A": (13, 5)}

        def bank(u, j=0):
            return 2 * (u % 2) + j

        def col(name, i, n=1):
            return cols[:, COLS[name][0] + i:COLS[name][0] + i + n]

        def streams(w):
            return range(w // LAT)

        def tokens(s):
            return slice(s * LAT, (s + 1) * LAT)

        def pairs(eng, n, body, first=False):
            lo = 1 if first else 0
            if first:
                body(0, False)
            if n - 1 > lo:
                with eng.Fori(lo, n - 1) as r:
                    body(r, False)
            body(n - 1, True)

        def up_dram(f, i):
            return t["w_up"][f, i]

        STEP_TILE = ((2, 3, 0, 1), (3, 2, 1, 0))
        ATT = [(tt, s, h2, qt) for tt in range(4) for s in range(2) for h2 in range(2) for qt in range(2)]
        OUTS = [(2, d, h) for d in range(2) for h in range(HM)] + [(3, d, h) for d in range(2) for h in range(HM)]
        STATES = [(s, d, h) for s in range(3) for d in range(2) for h in range(HM)]

        block = ctx.enter_context(nc.Block())

        @block.sync
        def _(sp):
            def load(u0, j, r, src, n):
                u = u0 + j + 2 * r
                if isinstance(r, int) and u < 2:
                    pass
                else:
                    sp.wait_ge(lo_made, u - 1)
                sp.dma_start(raw[:, (u0 + j) % 2, 0:n], src).then_inc(unit_in[(u0 + j) % 2], 16)

            sp.dma_start(c_in, t["c_in"]).then_inc(par_in, 16)
            sp.dma_start(sel[:], t["sel"]).then_inc(par_in, 16)
            sp.dma_start(mats[:], t["mats"]).then_inc(par_in, 16)
            sp.dma_start(mod_raw[:], t["mod_w"][0]).then_inc(mod_first[0], 16)
            sp.dma_start(cols[:], t["cols"]).then_inc(par_in, 16)
            sp.dma_start(xT[:], t["xT"]).then_inc(x_in, 16)
            sp.dma_start(mod_raw1[:], t["mod_w"][1]).then_inc(mod_first[1], 16)

            def ffn(f, name):
                at = 0
                for part, n in zip("AB", PARTS):
                    if name == "f0" and part == "A":
                        load(U["f0upA"], 0, 0, t["w_up"][f, 0], UNIT)
                        load(U["f0upA"], 1, 0, t["w_up"][f, 1], UNIT)
                        first = 1
                    else:
                        first = 0
                    with sp.Fori(first, n // 2) as r:
                        for j in range(2):
                            load(U[f"{name}up{part}"], j, r, t["w_up"][f, at + 2 * r + j], UNIT)
                    with sp.Fori(0, KT // 2) as r:
                        for j in range(2):
                            load(U[f"{name}down{part}"], j, r, t[f"w_down{part}"][f, 2 * r + j], n * P)
                    at += n

            ffn(0, "f0")
            for i in range(2):
                load(U["ev_in"] + i, 0, 0, t["w_ev_in"][i], UNIT)
            sp.wait_ge(unit_mm, U["ev_in"])
            sp.dma_start(cos_sin[:], t["cos_sin"]).then_inc(ev_in, 16)
            sp.dma_start(att_mask[:], t["att_mask"]).then_inc(ev_in, 16)
            for i in range(2, 7):
                load(U["ev_in"] + i, 0, 0, t["w_ev_in"][i], UNIT)
            for i in range(4):
                load(U["ev_out"] + i, 0, 0, t["w_ev_out"][i], UNIT)
            ffn(1, "f1")
            ffn(2, "f2")
            load(U["od_gate"], 0, 0, t["w_od_gate"], KT * 4 * HM)
            for i in range(16):
                load(U["od_in"] + i, 0, 0, t["w_od_in"][i], UNIT)
            for i in range(4):
                load(U["od_out"] + i, 0, 0, t["w_od_out"][i], UNIT)
            ffn(3, "f3")
            for k in range(KT):
                sp.wait_ge(y_made, k + 1)
                sp.dma_start(out[:, k, :], t_ring[:, k % 2, 0:LAT]).then_inc(y_out[k % 2], 16)
            for i in range(2):
                sp.wait_ge(y_out[i], 16 * KT // 2)

        @block.gpsimd
        def _(pool):
            pool.wait_ge(mod_mm, 1)
            pool.dma_start(mod_raw[:], t["mod_w"][2]).then_inc(mod_in, 16)
            with pool.Fori(3, JOBS) as m:
                pool.wait_ge(mod_mm, m)
                pool.dma_start(mod_raw[:], t["mod_w"][m]).then_inc(mod_in, 16)

        @block.tensor
        def _(pe):
            def three(o, lhs, rhs, first, last):
                (lh, ll), (rh, rl) = lhs, rhs
                pe.matmul(o, lh, rh, start=first, stop=False)
                pe.matmul(o, lh, rl, start=False, stop=False)
                return pe.matmul(o, ll, rh, start=False, stop=last)

            def weights(u0, a, b):
                return w_hi[:, u0 % 2, a:b], w_lo[:, u0 % 2, a:b]

            def begin(u, static=True):
                pe.wait_ge(lo_made, u + 1)
                if not static or u >= 2:
                    pe.wait_ge(unit_evac, u - 1)

            def unit(u0, r, nb, nk, w, operand, at, ready=None):
                begin(u0 + 2 * r, isinstance(r, int))
                for k in range(nk):
                    if ready:
                        ready(k)
                    for b in range(nb):
                        last = three(ps[:, bank(u0, b), 0:w], weights(u0, at(b, k), at(b, k) + P),
                                     (operand[0][:, k, 0:w], operand[1][:, k, 0:w]), k == 0, k == nk - 1)
                last.then_inc(unit_mm, 1)

            def mod_products(m, static):
                if static:
                    pe.wait_ge(mod_first[m], 16)
                else:
                    pe.wait_ge(mod_in, 16 * m - 16)
                source = mod_raw1 if static and m == 1 else mod_raw
                if not static or m > 0:
                    pe.wait_ge(mod_row, m)
                for k in range(KT):
                    for g in range(4):
                        last = pe.matmul(ps[32 * g:32 * g + 32, 4, 0:LAT], c_act[:, k, :],
                                         source[:, k, g * LAT:(g + 1) * LAT], start=(k == 0), stop=(k == KT - 1))
                last.then_inc(mod_mm, 1)

            def mod_columns(m, static):
                pe.wait_ge(mod_row, m + 1)
                if not static or m > 0:
                    pe.wait_ge(mod_made, m)
                for b in range(2):
                    last = pe.matmul(ps[:, 5, 8 * b:8 * b + 8], mrow[:, b * P:(b + 1) * P], sel[:],
                                     start=True, stop=True)
                last.then_inc(mod_tr, 1)

            def norm(n):
                pe.wait_ge(sq_added, KT * (n + 1))
                pe.matmul(ps[:, 6, 0:W[n]], ones, acc[:, 0:W[n]], start=True, stop=True).then_inc(norm_mm, 1)

            def hn_ready(n):
                return lambda k: pe.wait_ge(hn_made, KT * n + k + 1)

            def ffn(name, f, n, w):
                done = ABASE[name]
                for part, nf in zip("AB", PARTS):
                    up, down = U[f"{name}up{part}"], U[f"{name}down{part}"]
                    job, carry = JOB_OF.get(name + part, (0, 0))

                    def pair(r, end):
                        has = carry and (carry == nf // 2 or not end)
                        m = job + r
                        for j in range(2):
                            unit(up + j, r, 2, KT, w, (hn_hi, hn_lo), lambda b, k: b * KT * P + k * P,
                                 hn_ready(n) if isinstance(r, int) and r == 0 and j == 0 and part == "A" else None)
                            if has and j == 0:
                                mod_products(m, False)
                            if has and j == 1:
                                mod_columns(m, False)

                    pairs(pe, nf // 2, pair, True)
                    done += nf

                    def down_pair(r, end):
                        for j in range(2):
                            ready = None
                            if isinstance(r, int) and r == 0 and j == 0:
                                ready = lambda k: pe.wait_ge(a_made, done - nf + k + 1)
                            unit(down + j, r, 1, nf, w, (a_hi, a_lo), lambda b, k: k * P, ready)

                    pairs(pe, KT // 2, down_pair, True)

            pe.wait_ge(par_in, 64)
            pe.wait_ge(c_made, 1)
            for m in range(2):
                mod_products(m, True)
                mod_columns(m, True)
            norm(0)
            ffn("f0", 0, 0, TOK)
            norm(1)

            E = U["ev_in"]

            def two(b, k):
                return b * KT * P + k * P

            for c in range(CT):
                unit(E + c, 0, 2, KT, TOK, (hn_hi, hn_lo), two, hn_ready(1) if c == 0 else None)

            def rotate(i):
                pe.wait_ge(qk_raw, i + 1)
                if i >= 2:
                    pe.wait_ge(roped, i - 1)
                pe.matmul(ps[:, 6 + i % 2, 0:LAT], mat["rot"], qk[:, i, 0:LAT],
                          start=True, stop=True).then_inc(rot_mm, 1)

            unit(E + 4, 0, 2, KT, TOK, (hn_hi, hn_lo), two)
            unit(E + 5, 0, 2, KT, TOK, (hn_hi, hn_lo), two)
            rotate(0)
            rotate(1)
            u = E + 6
            begin(u)
            for k in range(KT):
                three(ps[:, bank(u), :], weights(u, k * P, (k + 1) * P), (hn_hi[:, k, :], hn_lo[:, k, :]),
                      k == 0, k == KT - 1)
            for i in range(4):
                for k in range(KT):
                    a = KT * P + k * P
                    last = three(ps[:, bank(u, 1), i * P:(i + 1) * P],
                                 (hn_hi[:, k, i * P:(i + 1) * P], hn_lo[:, k, i * P:(i + 1) * P]),
                                 weights(u, a, a + P), k == 0, k == KT - 1)
            last.then_inc(unit_mm, 1)
            for i in range(2, 5):
                rotate(i)

            pe.wait_ge(roped, 5)
            for c in range(CT):
                pe.wait_ge(conv_done, c + 1)
                last = pe.matmul(ps[:, 7, :], ones, y[:, c, :], start=(c == 0), stop=(c == CT - 1))
            last.then_inc(ln_mm, 1)
            for c in range(CT):
                pe.wait_ge(ln_sq, c + 1)
                pe.matmul(ps[:, 6, :], ones, sq[:, c % 2, :], start=(c == 0), stop=(c == CT - 1)).then_inc(ln_mm, 1)

            pe.wait_ge(roped, 5)
            pe.wait_ge(ln_ms, 1)

            def scores(j):
                tt, s, h2, qt = ATT[j]
                if j >= 2:
                    pe.wait_ge(exp_made, j - 1)
                k0 = LAT * s
                a = LAT * s + qt * P
                pe.matmul(ps[:, 4 + j % 2, k0:KEYS], qk[64 * h2:64 * h2 + 64, tt, a:a + P],
                          qk[64 * h2:64 * h2 + 64, CT, k0:KEYS], start=True, stop=True).then_inc(s_mm, 1)

            def turn(j):
                tt, s, h2, qt = ATT[j]
                pe.wait_ge(p_made, j + 1)
                if j >= 2:
                    pe.wait_ge(pT_made, j - 1)
                for kt in range(2 * s, 4):
                    last = pe.transpose(ps[:, 6 + j % 2, kt * P:(kt + 1) * P], prod[:, j % 2, kt * P:(kt + 1) * P],
                                        ident)
                last.then_inc(pT_mm, 1)

            def values(j):
                tt, s, h2, qt = ATT[j]
                g = j // 4
                pe.wait_ge(pT_made, j + 1)
                if g >= 2:
                    pe.wait_ge(mix_made, CT + g - 1)
                for kt in range(2 * s, 4):
                    last = pe.matmul(ps[64 * h2:64 * h2 + 64, g % 2, 0:LAT], v_att[:, kt, 64 * h2:64 * h2 + 64],
                                     pT[:, (j // 2) % 2, kt, :], start=(kt == 2 * s), stop=(kt == 3))
                last.then_inc(pv_mm, 1)

            NJ = len(ATT)
            for j in range(NJ + 3):
                if j < NJ:
                    scores(j)
                if 1 <= j < NJ + 1:
                    turn(j - 1)
                if j >= 3 and (j - 2) % 2 == 1 and j - 2 < NJ:
                    values(j - 2)

            for i in range(4):
                def ready(k):
                    pe.wait_ge(mix_made, k + 1 if k < CT else CT + 2 * (k - CT) + 2)
                unit(U["ev_out"] + i, 0, 2, KT, TOK, (hn_hi, hn_lo), two, ready if i == 0 else None)
            norm(2)
            ffn("f1", 1, 2, TOK)
            norm(3)
            ffn("f2", 2, 3, TOK)
            norm(4)

            u = U["od_gate"]
            begin(u)
            pe.wait_ge(hn_made, KT * 5)
            for i in range(4):
                for k in range(KT):
                    last = three(ps[:, bank(u), i * 16:(i + 1) * 16],
                                 (hn_hi[:, k, i * P:(i + 1) * P], hn_lo[:, k, i * P:(i + 1) * P]),
                                 weights(u, k * 16, (k + 1) * 16), k == 0, k == KT - 1)
            last.then_inc(unit_mm, 1)
            for n in range(8):
                u = U["od_in"] + n
                begin(u)
                for i in range(4):
                    for k in range(KT):
                        last = three(ps[:, bank(u, i // 2), (i % 2) * DH:(i % 2 + 1) * DH],
                                     (hn_hi[:, k, i * P:(i + 1) * P], hn_lo[:, k, i * P:(i + 1) * P]),
                                     weights(u, k * DH, (k + 1) * DH), k == 0, k == KT - 1)
                last.then_inc(unit_mm, 1)
                if n == 0:
                    pe.wait_ge(lf_made, 1)
                    lf = GATE["lf"].rearrange("p d s h -> p d (s h)")
                    pe.matmul(ps[:, 7, 0:16], mat["tri_up"], lf[:, 0, :], start=True, stop=True)
                    pe.matmul(ps[:, 7, 16:32], mat["tri_low"], lf[:, 1, :], start=True, stop=True)
                    pe.matmul(ps[:, 7, 32:64], ones, lf.rearrange("p d n -> p (d n)"), start=True, stop=True)\
                        .then_inc(cum_mm, 1)
                if 1 <= n <= 6:
                    for i in range(2 * n - 2, 2 * n):
                        pe.wait_ge(diag_made, i + 1)
                        pe.matmul(ps[:, 4 + i % 2, :], ones, sq[:, i % 2, :], start=True, stop=True).then_inc(diag_mm, 1)
            for n in range(8):
                unit(U["od_in"] + 8 + n, 0, 2, KT, LAT, (hn_hi, hn_lo), lambda b, k: k * DH + b * P)

            pe.wait_ge(hid_made, 4)
            for h in range(HM):
                pe.wait_ge(unit_evac, U["od_in"] + h + 1)
                if h >= 2:
                    pe.wait_ge(kT_made, h - 1)
                for kt in range(2):
                    for i in range(2):
                        last = pe.transpose(ps[:, 6 + h % 2, (2 * kt + i) * P:(2 * kt + i + 1) * P],
                                            k_tok[:, i, h, kt * P:(kt + 1) * P], ident)
                last.then_inc(kT_mm, 1)
            pe.wait_ge(unit_evac, U["od_in"] + 12)
            for i in range(2):
                for h in range(HM):
                    pe.wait_ge(kT_made, h + 1)
                    for kt in range(2):
                        last = pe.matmul(ps[:, 4 + i, h * P:(h + 1) * P], kT[:, 2 * h + kt, i * P:(i + 1) * P],
                                         qT[:, 2 * h + kt, i * P:(i + 1) * P], start=(kt == 0), stop=(kt == 1))
                last.then_inc(st_mm, 1)

            pe.wait_ge(unit_evac, U["od_out"])

            def state_up(n):
                s, d, h = STATES[n]
                pe.wait_ge(wk_made, n + 1)
                if n >= 2:
                    pe.wait_ge(st_made, n - 1)
                for kt in range(2):
                    last = pe.matmul(ps[:, 2 * (n % 2) + kt, 0:DH + 1], t_ring[:, n % 2, kt * P:(kt + 1) * P],
                                     v_tok[:, STEP_TILE[d][s], h, :], start=True, stop=True)
                last.then_inc(st_up, 1)

            def outputs(n):
                s, d, h = OUTS[n]
                i = STEP_TILE[d][s]
                if n == 0:
                    pe.wait_ge(sT_made, 4)
                if n >= 2:
                    pe.wait_ge(out_made, n - 1)
                pe.wait_ge(st_made, 8 * (s - 1) + HM * d + h + 1)
                pe.matmul(ps[:, 6 + n % 2, 0:DH + 1], decayed[:, s - 2, d, h, :], v_tok[:, i, h, :],
                          start=True, stop=True)
                for kt in range(2):
                    last = pe.matmul(ps[:, 4 + n % 2, 0:DH + 1], qT[:, 2 * h + kt, i * P:(i + 1) * P],
                                     state[:, d, h, kt, :], start=(kt == 0), stop=(kt == 1))
                last.then_inc(out_mm, 1)

            for n in range(16):
                state_up(n)
            for n in range(8):
                outputs(n)
            for n in range(8):
                state_up(16 + n)
            for n in range(8):
                outputs(8 + n)

            for h in range(HM):
                pe.wait_ge(hnorm, 8)
                if h >= 2:
                    pe.wait_ge(hz_made, h - 1)
                for kt in range(2):
                    for i in range(2):
                        last = pe.transpose(ps[:, 6 + h % 2, (2 * kt + i) * P:(2 * kt + i + 1) * P],
                                            xT[:, i * HM + h, LAT + kt * P:LAT + (kt + 1) * P], ident)
                last.then_inc(hT_mm, 1)
            for i in range(4):
                def ready(k):
                    pe.wait_ge(mix_made, CT + 8 + k // 2 + 1)
                unit(U["od_out"] + i, 0, 2, KT, LAT, (hn_hi, hn_lo), two, ready if i == 0 else None)
            norm(5)
            ffn("f3", 3, 5, LAT)
            norm(6)

        @block.scalar
        def _(act):
            linked = [0]

            def link(ins):
                linked[0] += 1
                ins.then_inc(link_s, 1)
                act.wait_ge(link_s, linked[0])

            def head(u0, r, n):
                u = u0 + 2 * r
                act.wait_ge(unit_in[u0 % 2], 16 * (u0 // 2 + 1) + 16 * r)
                if not (isinstance(r, int) and u < 2):
                    act.wait_ge(unit_mm, u - 1)
                act.activation(w_hi[:, u0 % 2, 0:n], raw[:, u0 % 2, 0:n], ACT.Copy).then_inc(hi_made, 1)

            def head_of(u):
                if u < NU:
                    head(u, 0, SIZE[u])

            def norm(n):
                w = W[n]
                act.preload_act_table(ACT.Sqrt)
                act.wait_ge(ms_made, n + 1)
                act.activation(sd[:, 0:w], sd[:, 0:w], ACT.Sqrt).then_inc(sd_made, 1)
                if n == 6:
                    return
                for k in range(KT):
                    act.wait_ge(t_made, KT * n + k + 1)
                    for s in streams(w):
                        last = act.activation(hn_hi[:, k, tokens(s)], t_ring[:, k % 2, tokens(s)], ACT.Identity,
                                              bias=modT[:, 3 * n, k, s:s + 1])
                    last.then_inc(hn_hi_made, 1)

            def mod_rows(m, static):
                act.wait_ge(mod_mm, m + 1)
                if not static or m > 0:
                    act.wait_ge(mod_tr, m)
                act.activation(mrow, ps[:, 4, 0:LAT], ACT.Copy).then_inc(mod_row, 1)

            def square_tile(n, u, d0, r, w):
                act.wait_ge(unit_evac, u + 1)
                act.wait_ge(sq_added, KT * n + d0 + 2 * r - 1)
                act.activation(sq[:, d0 % 2, 0:w], xT[:, d0 + 2 * r, 0:w], ACT.Square).then_inc(sq_made, 1)

            def ffn(name, f, n, w):
                tile = 0
                for part, nf in zip("AB", PARTS):
                    up, down = U[f"{name}up{part}"], U[f"{name}down{part}"]
                    job, carry = JOB_OF.get(name + part, (0, 0))
                    g0 = GBASE[name] + tile
                    a0 = ABASE[name] + tile

                    def pair(r, end):
                        has = carry and (carry == nf // 2 or not end)
                        for j in range(2):
                            if end:
                                head_of(up + j + 2 * r + 2)
                            else:
                                head(up + j + 2, r, UNIT)
                            act.wait_ge(unit_mm, up + j + 2 * r + 1)
                            act.activation(gact[:, j, 0:w], ps[:, bank(up + j, 0), 0:w], ACT.Silu).then_inc(gate_made, 1)
                            act.wait_ge(unit_evac, up + j + 2 * r + 1)
                            act.activation(a_hi[:, j + 2 * r, 0:w], prod[:, j, 0:w], ACT.Copy).then_inc(a_hi_made, 1)
                            if has and j == 0:
                                mod_rows(job + r, False)

                    act.preload_act_table(ACT.Silu)
                    pairs(act, nf // 2, pair)
                    tile += nf

                    def down_pair(r, end):
                        for j in range(2):
                            if not end:
                                head(down + j + 2, r, nf * P)
                            if part == "B":
                                square_tile(n + 1, down + j + 2 * r, j, r, w)
                            if end:
                                head_of(down + j + 2 * r + 2)

                    pairs(act, KT // 2, down_pair, part == "B")

            act.wait_ge(par_in, 64)
            act.activation(shared[:, LAT:2 * LAT], c_in, ACT.Silu).then_inc(c_made, 1)
            head_of(0)
            act.wait_ge(x_in, 16)
            for d in range(KT):
                if d >= 2:
                    act.wait_ge(sq_added, d - 1)
                act.activation(sq[:, d % 2, :], xT[:, d, :], ACT.Square).then_inc(sq_made, 1)
            head_of(1)
            for m in range(2):
                mod_rows(m, True)
            norm(0)
            ffn("f0", 0, 0, TOK)
            norm(1)

            E = U["ev_in"]
            for c in range(CT):
                head_of(E + c + 2)
                act.wait_ge(unit_mm, E + c + 1)
                act.activation(gact[:, c % 2, :], ps[:, bank(E + c, 1), :], ACT.Sigmoid).then_inc(gate_made, 1)
            for n in range(2):
                head_of(E + 6 + n)
                act.wait_ge(unit_mm, E + 5 + n)
                for b in range(2):
                    act.activation(qk[:, 2 * n + b, :], ps[:, bank(E + 4 + n, b), :], ACT.Copy).then_inc(qk_raw, 1)
            head_of(E + 8)
            act.wait_ge(unit_mm, E + 7)
            act.activation(v_att[:].rearrange("p a b -> p (a b)"), ps[:, bank(E + 6, 1), :], ACT.Copy)
            act.activation(qk[:, CT, :], ps[:, bank(E + 6), :], ACT.Copy).then_inc(qk_raw, 1)
            for c in range(CT):
                act.wait_ge(ln_cent, c + 1)
                if c >= 2:
                    act.wait_ge(ln_mm, c)
                act.activation(sq[:, c % 2, :], y[:, c, :], ACT.Square).then_inc(ln_sq, 1)
            act.wait_ge(ln_ms, 1)
            act.activation(sd[:], sd[:], ACT.Sqrt).then_inc(ln_sd, 1)
            for c in range(CT):
                act.wait_ge(ln_t, c + 1)
                link(act.activation(gact[:, c % 2, :], t_ring[:, c % 2, :], ACT.Silu, bias=col("ln_b", c)))
                act.activation(hn_hi[:, c, :], gact[:, c % 2, :], ACT.Copy).then_inc(ln_hi, 1)

            def expo(j):
                tt, s, h2, qt = ATT[j]
                act.wait_ge(max_made, j + 1)
                if j >= 2:
                    act.wait_ge(pT_mm, j - 1)
                src = ps[:, 4 + j % 2, LAT:KEYS] if s else gact[:, j % 2, :]
                neg = att_cols[:, 1, j:j + 1]
                act.activation(prod[:, j % 2, LAT * s:KEYS], src, ACT.Exp, bias=neg, scale=HD ** -0.5,
                               accum_out=att_cols[:, 2, j:j + 1])
                act.activation(att_cols[:, 3, j:j + 1], col("sink", tt + 4 * h2), ACT.Exp, bias=neg).then_inc(exp_made, 1)

            def turned(j):
                tt, s, h2, qt = ATT[j]
                act.wait_ge(pT_mm, j + 1)
                if j // 2 >= 2:
                    act.wait_ge(pv_mm, j // 2 - 1)
                act.activation(pT[:, (j // 2) % 2, 2 * s:4, qt * P:(qt + 1) * P],
                               ps[:, 6 + j % 2, 2 * s * P:4 * P].rearrange("p (k q) -> p k q", q=P),
                               ACT.Copy).then_inc(pT_made, 1)

            def att_head(g):
                act.wait_ge(pv_mm, 2 * g + 2)
                act.activation(hn_hi[:, CT + g // 2, tokens(g % 2)], ps[:, g % 2, 0:LAT], ACT.Copy).then_inc(att_hi, 1)

            NJ = len(ATT)
            for j in range(NJ + 2):
                if j < NJ:
                    expo(j)
                if 1 <= j < NJ + 1:
                    turned(j - 1)
                if j >= 5 and (j - 1) % 4 == 0:
                    att_head((j - 5) // 4)

            for i in range(4):
                u = U["ev_out"] + i
                if i < 2:
                    head_of(u + 2)
                act.wait_ge(unit_evac, u + 1)
                for b in range(2):
                    d = 2 * i + b
                    if d >= 2:
                        act.wait_ge(sq_added, KT * 2 + d - 1)
                    act.activation(sq[:, d % 2, :], xT[:, d, :], ACT.Square).then_inc(sq_made, 1)
            for i in range(2, 4):
                head_of(U["ev_out"] + i + 2)
            norm(2)
            ffn("f1", 1, 2, TOK)
            norm(3)
            ffn("f2", 2, 3, TOK)
            norm(4)

            head_of(U["od_gate"] + 2)
            act.wait_ge(g_in, 1)
            link(act.activation(GATE["abs"], GATE["f"], ACT.Abs))
            link(act.activation(GATE["exp"], GATE["abs"], ACT.Exp, scale=-1.0))
            act.activation(GATE["ln"], GATE["exp"], ACT.Ln, bias=1.0).then_inc(ln1p, 1)
            for n in range(5):
                head_of(U["od_in"] + 2 + n)
            act.wait_ge(arg_made, 1)
            act.activation(GATE["val"][:, :, 0:3, :], GATE["arg"][:, :, 0:3, :], ACT.Exp)
            act.activation(GATE["mm"][:, :, 1:3, :], GATE["exp"][:, :, 1:3, :], ACT.Exp)
            act.activation(GATE["lf"][:, :, 2:4, :], GATE["ln"][:, :, 2:4, :], ACT.Exp)
            act.activation(GATE["cmax"][:, :, 2:4, :], GATE["f"][:, :, 2:4, :], ACT.Exp, scale=-1.0).then_inc(val_made, 1)
            head_of(U["od_in"] + 7)
            for i in range(4):
                s, d = 2 + i // 2, i % 2
                act.wait_ge(hid_made, i + 1)
                for h in range(HM):
                    last = act.activation(decayed[:, s - 2, d, h, :], t_ring[:, i % 2, h * P:(h + 1) * P], ACT.Exp,
                                          bias=GATE["a"][:, d, s, h:h + 1], scale=-1.0)
                last.then_inc(dec_made, 1)
            for n in range(6, 16):
                if n + 2 >= 8:
                    head_of(U["od_in"] + n + 2)
                if n >= 12:
                    act.wait_ge(unit_mm, U["od_in"] + n + 1)
                    for b in range(2):
                        last = act.activation(gact[:, n % 2, b * LAT:(b + 1) * LAT],
                                              ps[:, bank(U["od_in"] + n, b), 0:LAT], ACT.Sigmoid)
                    last.then_inc(gate_made, 1)
            for h in range(HM):
                act.wait_ge(kT_mm, h + 1)
                act.activation(kT[:, 2 * h:2 * h + 2, :], ps[:, 6 + h % 2, :].rearrange("p (a b) -> p a b", a=2),
                               ACT.Copy).then_inc(kT_made, 1)
            for n in range(16):
                s, d, h = OUTS[n]
                act.wait_ge(out_mm, n + 1)
                act.activation(gact[:, n % 2, 0:DH + 1], ps[:, 4 + n % 2, 0:DH + 1], ACT.Copy,
                               scale=GATE["lf"][:, d, s, h:h + 1]).then_inc(out_scaled, 1)
            act.wait_ge(h_made, 16)
            for i in range(8):
                last = act.activation(sq[:, i % 2, 0:DH] if i < 2 else prod[:, i % 2, 0:DH] if i < 4 else
                                      gact[:, i % 2, 0:DH] if i < 6 else rstd[:, (i % 2) * DH:(i % 2 + 1) * DH],
                                      xT[:, i, LAT:TOK], ACT.Square, accum_out=ms_cols[:, 0, i:i + 1])
            last.then_inc(ss_made, 1)
            act.wait_ge(hms_made, 1)
            act.activation(ms_cols[:, 1, :], ms_cols[:, 1, :], ACT.Sqrt).then_inc(hsd_made, 1)
            for h in range(HM):
                act.wait_ge(hz_made, h + 1)
                act.activation(hn_hi[:, 2 * h:2 * h + 2, 0:LAT], prod[:, h % 2, :].rearrange("p (a b) -> p a b", a=2),
                               ACT.Copy).then_inc(hz_hi, 1)
            for i in range(4):
                u = U["od_out"] + i
                if i < 2:
                    head_of(u + 2)
                act.wait_ge(unit_evac, u + 1)
                for b in range(2):
                    d = 2 * i + b
                    act.wait_ge(sq_added, KT * 5 + d - 1)
                    act.activation(sq[:, d % 2, 0:LAT], xT[:, d, 0:LAT], ACT.Square).then_inc(sq_made, 1)
            for i in range(2, 4):
                head_of(U["od_out"] + i + 2)
            norm(5)
            ffn("f3", 3, 5, LAT)
            norm(6)

        @block.vector
        def _(dve):
            linked = [0]

            def link(ins):
                linked[0] += 1
                ins.then_inc(link_v, 1)
                dve.wait_ge(link_v, linked[0])

            def rest(u0, r, n):
                dve.wait_ge(hi_made, u0 + 2 * r + 1)
                dve.tensor_tensor(w_lo[:, u0 % 2, 0:n], raw[:, u0 % 2, 0:n], w_hi[:, u0 % 2, 0:n],
                                  ALU.subtract).then_inc(lo_made, 1)

            def rest_of(u):
                if u < NU:
                    rest(u, 0, SIZE[u])

            def add_square(n, d0, r, w):
                before = KT * n + d0 + 2 * r
                dve.wait_ge(sq_made, before + 1)
                if not (isinstance(r, int) and n == 0 and d0 + 2 * r == 0):
                    dve.wait_ge(sq_added, before)
                dve.tensor_tensor(acc[:, 0:w], acc[:, 0:w], sq[:, d0 % 2, 0:w], ALU.add).then_inc(sq_added, 1)

            def residual(u0, b, r, d0, vec, w):
                for s in streams(w):
                    last = dve.scalar_tensor_tensor(
                        out=xT[:, d0 + 2 * r, tokens(s)], in0=ps[:, bank(u0, b), tokens(s)],
                        scalar=modT[:, vec, d0 + 2 * r, s:s + 1], in1=xT[:, d0 + 2 * r, tokens(s)],
                        op0=ALU.mult, op1=ALU.add)
                return last

            def norm(n):
                w = W[n]
                name, at = GAIN[n]
                if n < 6:
                    dve.wait_ge(mod_made, 3 * n + 2)
                    for s in range(2):
                        last = dve.scalar_tensor_tensor(out=modT[:, 3 * n + 1, :, s], in0=modT[:, 3 * n + 1, :, s],
                                                        scalar=1.0, in1=col(name, at, KT), op0=ALU.add, op1=ALU.mult)
                    link(last)
                dve.wait_ge(norm_mm, n + 1)
                dve.tensor_scalar(sd[:, 0:w], ps[:, 6, 0:w], 1.0 / D, EPS, ALU.mult, ALU.add).then_inc(ms_made, 1)
                dve.memset(acc[:], 0.0).then_inc(acc_clear, 1)
                dve.wait_ge(acc_clear, n + 2)
                dve.wait_ge(sd_made, n + 1)
                dve.reciprocal(rstd[:, 0:w], sd[:, 0:w]).then_inc(rstd_made, 1)
                dve.wait_ge(rstd_made, n + 1)

                def scaled(k):
                    if k >= 2 and n < 6:
                        dve.wait_ge(hn_made, KT * n + k - 1)
                    for s in streams(w):
                        gain = modT[:, 3 * n + 1, k, s:s + 1] if n < 6 else col(name, k)
                        last = dve.scalar_tensor_tensor(out=t_ring[:, k % 2, tokens(s)], in0=xT[:, k, tokens(s)],
                                                        scalar=gain, in1=rstd[:, tokens(s)], op0=ALU.mult, op1=ALU.mult)
                    last.then_inc(t_made if n < 6 else y_made, 1)

                if n == 6:
                    for k in range(KT):
                        if k >= 2:
                            dve.wait_ge(y_out[k % 2], 16 * (k // 2))
                        scaled(k)
                    return
                scaled(0)
                for k in range(KT):
                    if k + 1 < KT:
                        scaled(k + 1)
                    dve.wait_ge(hn_hi_made, KT * n + k + 1)
                    for s in streams(w):
                        last = dve.scalar_tensor_tensor(out=hn_lo[:, k, tokens(s)], in0=t_ring[:, k % 2, tokens(s)],
                                                        scalar=modT[:, 3 * n, k, s:s + 1], in1=hn_hi[:, k, tokens(s)],
                                                        op0=ALU.add, op1=ALU.subtract)
                    last.then_inc(hn_made, 1)

            def mod_vector(m):
                dve.wait_ge(mod_tr, m + 1)
                bias = cols[:, COLS["mod_b"][0]:COLS["mod_b"][0] + JOBS * KT].rearrange(
                    "p (m g b) -> p m b g", m=JOBS, b=2)
                to = modT[:].rearrange("p m (g b) s -> p m b g s", b=2)
                for b in range(2):
                    for s in range(2):
                        last = dve.tensor_tensor(to[:, m, b, :, s],
                                                 ps[:, 5, 8 * b:8 * b + 8].rearrange("p (g s) -> p g s", s=2)[:, :, s],
                                                 bias[:, m, b, :], ALU.add)
                last.then_inc(mod_made, 1)

            def ffn(name, f, n, w):
                tile = 0
                vec = 3 * n + 2
                for part, nf in zip("AB", PARTS):
                    up, down = U[f"{name}up{part}"], U[f"{name}down{part}"]
                    job, carry = JOB_OF.get(name + part, (0, 0))
                    g0 = GBASE[name] + tile
                    a0 = ABASE[name] + tile

                    def pair(r, end):
                        has = carry and (carry == nf // 2 or not end)
                        for j in range(2):
                            if end:
                                rest_of(up + j + 2 * r + 2)
                            else:
                                rest(up + j + 2, r, UNIT)
                            dve.wait_ge(gate_made, g0 + j + 2 * r + 1)
                            if not (isinstance(r, int) and a0 + j + 2 * r == 0):
                                dve.wait_ge(a_made, a0 + j + 2 * r)
                            dve.tensor_tensor(prod[:, j, 0:w], gact[:, j, 0:w], ps[:, bank(up + j, 1), 0:w],
                                              ALU.mult).then_inc(unit_evac, 1)
                            dve.wait_ge(a_hi_made, a0 + j + 2 * r + 1)
                            dve.tensor_tensor(a_lo[:, j + 2 * r, 0:w], prod[:, j, 0:w], a_hi[:, j + 2 * r, 0:w],
                                              ALU.subtract).then_inc(a_made, 1)
                            if has and j == 1:
                                mod_vector(job + r)

                    pairs(dve, nf // 2, pair, a0 == 0)
                    if part == "A":
                        dve.wait_ge(mod_made, vec + 1)
                        link(dve.tensor_scalar(modT[:, vec, :, :], modT[:, vec, :, :], 0.5, None, ALU.mult))
                    tile += nf

                    def down_pair(r, end):
                        for j in range(2):
                            dve.wait_ge(unit_mm, down + j + 2 * r + 1)
                            residual(down + j, 0, r, j, vec, w).then_inc(unit_evac, 1)
                            if not end:
                                rest(down + j + 2, r, nf * P)
                            if part == "B":
                                add_square(n + 1, j, r, w)
                            if end:
                                rest_of(down + j + 2 * r + 2)

                    pairs(dve, KT // 2, down_pair)

            dve.memset(acc[:], 0.0).then_inc(acc_clear, 1)
            dve.wait_ge(par_in, 64)
            dve.wait_ge(acc_clear, 1)
            rest_of(0)
            for d in range(KT):
                add_square(0, d, 0, TOK)
            rest_of(1)
            for m in range(2):
                mod_vector(m)
            norm(0)
            ffn("f0", 0, 0, TOK)
            norm(1)

            E = U["ev_in"]
            dve.memset(upad[:, :, :, 0:PAD], 0.0)
            dve.memset(upad[:, :, :, PAD + LAT:PADDED], 0.0).then_inc(pad_clear, 1)
            dve.wait_ge(pad_clear, 1)
            two_streams = lambda ap: ap.rearrange("p (s n) -> p s n", s=2)
            for c in range(CT):
                rest_of(E + c + 2)
                dve.wait_ge(gate_made, CONV_G + c + 1)
                dve.tensor_tensor(upad[:, c, :, PAD:PAD + LAT], two_streams(gact[:, c % 2, :]),
                                  two_streams(ps[:, bank(E + c), :]), ALU.mult).then_inc(unit_evac, 1)
                dve.wait_ge(unit_evac, E + c + 1)
                dst = two_streams(y[:, c, :])
                for i in range(CONV_W):
                    src = upad[:, c, :, i:i + LAT]
                    if i == 0:
                        ins = dve.tensor_scalar(dst, src, col("conv_w", c), col("conv_b", c), ALU.mult, ALU.add)
                    else:
                        ins = dve.scalar_tensor_tensor(out=dst, in0=src, scalar=col("conv_w", i * CT + c), in1=dst,
                                                       op0=ALU.mult, op1=ALU.add)
                    if i < CONV_W - 1:
                        ins.then_inc(tap_done, 1)
                        dve.wait_ge(tap_done, c * (CONV_W - 1) + i + 1)
                ins.then_inc(conv_done, 1)

            def turn_part(i):
                n = i // 2
                if i >= 2:
                    dve.wait_ge(roped, i - 1)
                dve.tensor_tensor(t_ring[:, i % 2, 0:LAT], ps[:, bank(E + 4 + n, i % 2), 0:LAT], cos_sin[:, 0, :],
                                  ALU.mult).then_inc(*((unit_evac, 1) if i % 2 or i == 4 else (tap_done, 1)))

            def rope(i):
                dve.wait_ge(rot_mm, i + 1)
                link(dve.tensor_tensor(sq[:, i % 2, 0:LAT], ps[:, 6 + i % 2, 0:LAT],
                                       cos_sin[:, 1, :], ALU.mult))
                dve.tensor_tensor(qk[:, i, 0:LAT], t_ring[:, i % 2, 0:LAT], sq[:, i % 2, 0:LAT],
                                  ALU.add).then_inc(roped, 1)

            dve.wait_ge(ev_in, 32)
            for n in range(3):
                rest_of(E + 6 + n)
                for i in range(2 * n, min(2 * n + 2, 5)):
                    dve.wait_ge(qk_raw, i + 1)
                    turn_part(i)
                for i in range(2 * n, min(2 * n + 2, 5)):
                    rope(i)

            dve.wait_ge(ln_mm, 1)
            link(dve.tensor_scalar(sd[:], ps[:, 7, :], 1.0 / (CT * P), None, ALU.mult))
            for c in range(CT):
                dve.tensor_tensor(y[:, c, :], y[:, c, :], sd[:], ALU.subtract).then_inc(ln_cent, 1)
            dve.wait_ge(ln_mm, 1 + CT)
            dve.tensor_scalar(sd[:], ps[:, 6, :], 1.0 / (CT * P), EPS, ALU.mult, ALU.add).then_inc(ln_ms, 1)
            dve.wait_ge(ln_sd, 1)
            link(dve.reciprocal(rstd[:], sd[:]))

            def ln_scaled(c):
                dve.scalar_tensor_tensor(out=t_ring[:, c % 2, :], in0=y[:, c, :], scalar=col("ln_g", c), in1=rstd[:],
                                         op0=ALU.mult, op1=ALU.mult).then_inc(ln_t, 1)

            ln_scaled(0)
            for c in range(CT):
                if c + 1 < CT:
                    ln_scaled(c + 1)
                dve.wait_ge(ln_hi, c + 1)
                dve.tensor_tensor(hn_lo[:, c, :], gact[:, c % 2, :], hn_hi[:, c, :], ALU.subtract).then_inc(mix_made, 1)

            link(dve.tensor_scalar(att_cols[:, 4, 0:NH_ATT], col("sink", 0, NH_ATT), -1.0, None, ALU.mult))

            def largest(j):
                tt, s, h2, qt = ATT[j]
                dve.wait_ge(s_mm, j + 1)
                top = att_cols[:, 0, j:j + 1]
                if s == 0:
                    link(dve.tensor_tensor_reduce(out=gact[:, j % 2, :], in0=ps[:, 4 + j % 2, :], in1=att_mask[:, qt, :],
                                                  scale=1.0, scalar=-3e38, op0=ALU.add, op1=ALU.max, accum_out=top))
                else:
                    link(dve.reduce_max(top, ps[:, 4 + j % 2, LAT:KEYS], AX.X))
                head = tt + 4 * h2
                dve.tensor_scalar(att_cols[:, 1, j:j + 1], top, -HD ** -0.5, att_cols[:, 4, head:head + 1],
                                  ALU.mult, ALU.min).then_inc(max_made, 1)

            def normalise(j):
                tt, s, h2, qt = ATT[j]
                dve.wait_ge(exp_made, j + 1)
                den = att_cols[:, 5, j:j + 1]
                link(dve.tensor_tensor(den, att_cols[:, 2, j:j + 1], att_cols[:, 3, j:j + 1], ALU.add))
                link(dve.reciprocal(den, den))
                p = prod[:, j % 2, LAT * s:KEYS]
                dve.tensor_scalar(p, p, den, None, ALU.mult).then_inc(p_made, 1)

            NJ = len(ATT)
            for j in range(NJ + 3):
                if j < NJ:
                    largest(j)
                if 1 <= j < NJ + 1:
                    normalise(j - 1)
                if j >= 6 and (j - 2) % 4 == 0:
                    g = (j - 6) // 4
                    dve.wait_ge(att_hi, g + 1)
                    dve.tensor_tensor(hn_lo[:, CT + g // 2, tokens(g % 2)], ps[:, g % 2, 0:LAT],
                                      hn_hi[:, CT + g // 2, tokens(g % 2)], ALU.subtract).then_inc(mix_made, 1)

            def mix_out(name, n, w):
                for i in range(4):
                    u = U[name] + i
                    dve.wait_ge(unit_mm, u + 1)
                    residual(u, 0, 0, 2 * i, 3 * n - 1, w)
                    residual(u, 1, 0, 2 * i + 1, 3 * n - 1, w).then_inc(unit_evac, 1)
                    if i < 2:
                        rest_of(u + 2)
                    for b in range(2):
                        add_square(n, 2 * i + b, 0, w)
                for i in range(2, 4):
                    rest_of(U[name] + i + 2)

            mix_out("ev_out", 2, TOK)
            norm(2)
            ffn("f1", 1, 2, TOK)
            norm(3)
            ffn("f2", 2, 3, TOK)
            norm(4)

            u = U["od_gate"]
            rest_of(u + 2)
            dve.wait_ge(unit_mm, u + 1)
            for d in range(2):
                for s in range(4):
                    i = STEP_TILE[d][s]
                    for kind, name in enumerate(("li", "f")):
                        a = 8 * d + HM * kind
                        last = dve.tensor_tensor(GATE[name][:, d, s, :], ps[:, bank(u), i * 16 + a:i * 16 + a + HM],
                                                 col("b_gate", a, HM), ALU.add)
            last.then_inc(unit_evac, 1)
            dve.memset(v_tok[:, :, :, DH:DH + 1], 1.0).then_inc(g_in, 1)
            dve.wait_ge(ln1p, 1)
            dve.scalar_tensor_tensor(out=GATE["lf"], in0=GATE["f"], scalar=0.0, in1=GATE["ln"], op0=ALU.min,
                                     op1=ALU.subtract).then_inc(lf_made, 1)

            def flat(ap):
                return ap.rearrange("p d s h -> p (d s h)")

            def spread(i, values):
                if i >= 2:
                    dve.wait_ge(diag_mm, i - 1)
                dve.tensor_tensor(sq[:, i % 2, :].rearrange("p (h n) -> p h n", h=HM),
                                  ident.unsqueeze(1).to_broadcast([P, HM, P]),
                                  values.unsqueeze(2).to_broadcast([P, HM, P]), ALU.mult).then_inc(diag_made, 1)

            def diagonal(i):
                if i < 8:
                    spread(i, GATE["a"][:, i // 4, i % 4, :])
                else:
                    spread(i, GATE["mq"][:, i % 2, 2 + (i - 8) // 2, :])

            def four(ap):
                return ap.rearrange("p (h n) -> p h n", h=HM)

            def maxima(i):
                d, s = i // 4, i % 4
                dve.wait_ge(diag_mm, i + 1)
                bk = four(ps[:, 4 + i % 2, :])
                if s >= 2:
                    hide = mat["hide_after" if d == 0 else "hide_before"]
                    link(dve.tensor_tensor(four(t_ring[:, i % 2, :]), bk, hide.unsqueeze(1).to_broadcast([P, HM, P]),
                                           ALU.add))
                    ins = dve.tensor_reduce(GATE["cmax"][:, d, s, :], four(t_ring[:, i % 2, :]), AX.X, ALU.max)
                    if s == 3:
                        ins.then_inc(diag_free, 1)
                        return
                dve.tensor_reduce(GATE["amax"][:, d, s, :], bk, AX.X, ALU.max).then_inc(diag_free, 1)

            def hidden(i):
                d = i % 2
                dve.wait_ge(diag_mm, 8 + i + 1)
                if i >= 2:
                    dve.wait_ge(dec_made, i - 1)
                hide = mat["hide_before" if d == 0 else "hide_after"]
                dve.tensor_tensor(four(t_ring[:, i % 2, :]), four(ps[:, 4 + i % 2, :]),
                                  hide.unsqueeze(1).to_broadcast([P, HM, P]), ALU.subtract).then_inc(hid_made, 1)

            def chain():
                g = GATE
                link(dve.memset(g["m"][:, :, 0, :], 0.0))
                for s in range(3):
                    link(dve.tensor_tensor(g["mm"][:, :, s, :], g["m"][:, :, s, :], g["amax"][:, :, s, :], ALU.max))
                    link(dve.tensor_tensor(g["m"][:, :, s + 1, :], g["end"][:, :, s, :], g["mm"][:, :, s, :], ALU.add))
                link(dve.tensor_tensor(g["mq"][:, :, 2:4, :], g["cmax"][:, :, 2:4, :], g["m"][:, :, 2:4, :], ALU.max))
                dve.tensor_tensor(g["arg"][:, :, 0:3, :], g["a"][:, :, 0:3, :], g["mm"][:, :, 0:3, :], ALU.subtract)
                dve.tensor_tensor(g["f"][:, :, 2:4, :], g["b"][:, :, 2:4, :], g["mq"][:, :, 2:4, :], ALU.add)
                dve.tensor_tensor(g["exp"][:, :, 0:3, :], g["m"][:, :, 0:3, :], g["mm"][:, :, 0:3, :], ALU.subtract)
                dve.tensor_tensor(g["ln"][:, :, 2:4, :], g["m"][:, :, 2:4, :], g["mq"][:, :, 2:4, :],
                                  ALU.subtract).then_inc(arg_made, 1)

            for n in range(16):
                u = U["od_in"] + n
                if n != 6:
                    rest_of(u + 2)
                dve.wait_ge(unit_mm, u + 1)
                h = n % 4
                if n < 4:
                    for b in range(2):
                        last = dve.tensor_scalar(k_tok[:, 2 * b:2 * b + 2, h, :], two_streams(ps[:, bank(u, b), :]),
                                                 DH ** -0.5, None, ALU.mult)
                elif n < 8:
                    for b in range(2):
                        last = dve.tensor_copy(v_tok[:, 2 * b:2 * b + 2, h, 0:DH], two_streams(ps[:, bank(u, b), :]))
                elif n < 12:
                    for b in range(2):
                        last = dve.tensor_copy(qT[:, 2 * h + b, :], ps[:, bank(u, b), 0:LAT])
                else:
                    dve.wait_ge(gate_made, OD_G + h + 1)
                    for b in range(2):
                        last = dve.tensor_scalar(oT[:, 2 * h + b, :], gact[:, n % 2, b * LAT:(b + 1) * LAT],
                                                 col("norm_g", 2 * h + b), None, ALU.mult)
                last.then_inc(unit_evac, 1)
                if n == 0:
                    dve.wait_ge(cum_mm, 1)
                    dve.tensor_copy(flat(GATE["b"]), ps[:, 7, 0:32])
                    dve.tensor_copy(flat(GATE["end"]), ps[:, 7, 32:64])
                    link(dve.tensor_tensor(flat(GATE["a"]), flat(GATE["li"]), ps[:, 7, 0:32], ALU.subtract))
                    diagonal(0)
                    diagonal(1)
                if 1 <= n <= 4:
                    for i in range(2 * n - 2, 2 * n):
                        maxima(i)
                        if i + 2 < 8:
                            diagonal(i + 2)
                if n == 4:
                    chain()
                    diagonal(8)
                    diagonal(9)
                if n == 5:
                    hidden(0)
                    diagonal(10)
                    hidden(1)
                    diagonal(11)
                if n == 6:
                    hidden(2)
                    hidden(3)
                    rest_of(u + 2)

            for i in range(4):
                s, d = 2 + i // 2, i % 2
                dve.wait_ge(dec_made, i + 1)
                dve.wait_ge(st_mm, STEP_TILE[d][s] + 1)
                dve.tensor_tensor(decayed[:, s - 2, d], decayed[:, s - 2, d], four(ps[:, 4 + STEP_TILE[d][s], :]),
                                  ALU.mult).then_inc(sT_made, 1)
            dve.wait_ge(val_made, 1)

            def weighted(n):
                s, d, h = STATES[n]
                if n >= 2:
                    dve.wait_ge(st_up, n - 1)
                dve.tensor_scalar(t_ring[:, n % 2, 0:DH], k_tok[:, STEP_TILE[d][s], h, :],
                                  GATE["val"][:, d, s, h:h + 1], None, ALU.mult).then_inc(wk_made, 1)

            def new_state(n):
                s, d, h = STATES[n]
                dve.wait_ge(st_up, n + 1)
                for kt in range(2):
                    src = ps[:, 2 * (n % 2) + kt, 0:DH + 1]
                    if s == 0:
                        last = dve.tensor_copy(state[:, d, h, kt, :], src)
                    else:
                        last = dve.scalar_tensor_tensor(out=state[:, d, h, kt, :], in0=state[:, d, h, kt, :],
                                                        scalar=GATE["mm"][:, d, s, h:h + 1], in1=src,
                                                        op0=ALU.mult, op1=ALU.add)
                last.then_inc(st_made, 1)

            def head_output(n):
                s, d, h = OUTS[n]
                i = STEP_TILE[d][s]
                dve.wait_ge(out_scaled, n + 1)
                total = prod[:, n % 2, 0:DH + 1]
                dve.tensor_tensor(total, gact[:, n % 2, 0:DH + 1], ps[:, 6 + n % 2, 0:DH + 1],
                                  ALU.add).then_inc(out_made, 1)
                dve.wait_ge(out_made, n + 1)
                den = out_cols[:, 0, n:n + 1]
                whole = total[:, DH:DH + 1]
                link(dve.scalar_tensor_tensor(out=den, in0=whole, scalar=-1.0, in1=whole, op0=ALU.mult, op1=ALU.max))
                link(dve.tensor_tensor(den, den, GATE["cmax"][:, d, s, h:h + 1], ALU.max))
                link(dve.reciprocal(den, den))
                dst = xT[:, i * HM + h, LAT:TOK]
                if s == 2:
                    dve.tensor_scalar(dst, total[:, 0:DH], den, None, ALU.mult).then_inc(h_made, 1)
                else:
                    dve.scalar_tensor_tensor(out=dst, in0=total[:, 0:DH], scalar=den, in1=dst, op0=ALU.mult,
                                             op1=ALU.add).then_inc(h_made, 1)

            def states(a, b):
                weighted(a)
                for n in range(a, b):
                    if n + 1 < b:
                        weighted(n + 1)
                    new_state(n)

            states(0, 16)
            for n in range(8):
                head_output(n)
            states(16, 24)
            for n in range(8, 16):
                head_output(n)

            dve.wait_ge(ss_made, 1)
            dve.tensor_scalar(ms_cols[:, 1, :], ms_cols[:, 0, :], 1.0 / DH, EPS, ALU.mult, ALU.add).then_inc(hms_made, 1)
            dve.wait_ge(hsd_made, 1)
            link(dve.reciprocal(ms_cols[:, 1, :], ms_cols[:, 1, :]))
            for i in range(8):
                dve.tensor_scalar(xT[:, i, LAT:TOK], xT[:, i, LAT:TOK], ms_cols[:, 1, i:i + 1], None,
                                  ALU.mult).then_inc(hnorm, 1)

            def gated(h):
                dve.wait_ge(hT_mm, h + 1)
                if h >= 2:
                    dve.wait_ge(mix_made, CT + 8 + h - 1)
                dve.tensor_tensor(two_streams(prod[:, h % 2, :]), two_streams(ps[:, 6 + h % 2, :]),
                                  oT[:, 2 * h:2 * h + 2, :], ALU.mult).then_inc(hz_made, 1)

            gated(0)
            for h in range(HM):
                if h + 1 < HM:
                    gated(h + 1)
                dve.wait_ge(hz_hi, h + 1)
                dve.tensor_tensor(hn_lo[:, 2 * h:2 * h + 2, 0:LAT], two_streams(prod[:, h % 2, :]),
                                  hn_hi[:, 2 * h:2 * h + 2, 0:LAT], ALU.subtract).then_inc(mix_made, 1)
            mix_out("od_out", 5, LAT)
            norm(5)
            ffn("f3", 3, 5, LAT)
            norm(6)


def columns(a):
    return np.ascontiguousarray(a).reshape(-1, P).T


def tiles(w, width):
    k, n = w.shape
    return w.reshape(k // P, P, n // width, width).transpose(2, 1, 0, 3).reshape(n // width, P, -1)


def shape_constants():
    i = np.arange(P)
    up = (i[:, None] <= i[None, :]).astype(np.float32)
    rot = np.zeros((P, P), np.float32)
    for a in range(0, P, 2 * ROPE_FREQS):
        for j in range(ROPE_FREQS):
            rot[a + ROPE_FREQS + j, a + j] = -1.0
            rot[a + j, a + ROPE_FREQS + j] = 1.0
    mats = {
        "ident": np.eye(P, dtype=np.float32),
        "ones": np.ones((P, P), np.float32),
        "tri_up": up,
        "tri_low": np.ascontiguousarray(up.T),
        "hide_after": np.where(i[None, :] > i[:, None], np.float32(-BIG), np.float32(0)),
        "hide_before": np.where(i[None, :] < i[:, None], np.float32(-BIG), np.float32(0)),
        "rot": rot,
    }
    tok = np.arange(LAT)
    place = np.stack([tok // GRID_W, tok % GRID_W]).astype(np.float32)
    inv = np.float32(10000.0) ** (-np.arange(ROPE_FREQS, dtype=np.float32) / np.float32(ROPE_FREQS))
    feature = np.arange(P) % HD
    angle = place[feature // (2 * ROPE_FREQS)] * inv[feature % ROPE_FREQS][:, None]
    cos_sin = np.stack([np.cos(angle), np.sin(angle)], axis=1).astype(np.float32)
    query = np.arange(P)[:, None, None] + P * np.arange(2)[None, :, None]
    key = np.arange(KEYS)[None, None, :]
    hidden = (key < LAT) & (np.abs(key - query) > WINDOW)
    mask = np.where(hidden, np.float32(-BIG), np.float32(0))
    sel = np.zeros((P, 8), np.float32)
    for g in range(4):
        for s in range(2):
            sel[32 * g + s, 2 * g + s] = 1.0
    return {"mats": np.stack([mats[n] for n in MATS], axis=1), "cos_sin": cos_sin, "att_mask": mask, "sel": sel}


def layout(x, c, ctx, c_ctx, mod_w, mod_b, ffn1_norm, ffn1_w_gu, ffn1_w_d, mix_norm, ffn2_norm, ffn2_w_gu,
           ffn2_w_d, ev_w_in, ev_conv_w, ev_conv_b, ev_conv_ln_g, ev_conv_ln_b, ev_sink, ev_w_out, od_w_in,
           od_b_gate, od_norm_g, od_w_out, final_norm):
    put = shape_constants()
    put["xT"] = np.concatenate([x[0], ctx[0]], axis=0).T.reshape(KT, P, TOK).transpose(1, 0, 2)
    cond = np.zeros((P, KT, 32), np.float32)
    cond[:, :, 0] = columns(c)
    cond[:, :, 1] = columns(c_ctx)
    put["c_in"] = cond.reshape(P, KT * 32)
    put["cols"] = np.concatenate(
        [columns(ffn1_norm), columns(mix_norm), columns(ffn2_norm), columns(final_norm), columns(ev_conv_b),
         columns(ev_conv_ln_g), columns(ev_conv_ln_b), columns(od_norm_g), columns(ev_conv_w), columns(mod_b),
         np.broadcast_to(ev_sink.reshape(1, -1), (P, NH_ATT)), np.broadcast_to(od_b_gate.reshape(1, -1), (P, 4 * HM))],
        axis=1)
    put["mod_w"] = mod_w.reshape(2, KT, P, NVEC, D).transpose(0, 3, 2, 1, 4).reshape(JOBS, P, KT, D)
    ups = [ffn1_w_gu[0], ffn2_w_gu[0], ffn1_w_gu[1], ffn2_w_gu[1]]
    downs = [ffn1_w_d[0], ffn2_w_d[0], ffn1_w_d[1], ffn2_w_d[1]]
    put["w_up"] = np.stack([w.reshape(KT, P, 2, FT, P).transpose(3, 1, 2, 0, 4).reshape(FT, P, UNIT) for w in ups])
    cut = PARTS[0] * P
    put["w_downA"] = np.stack([tiles(w[:cut], P) for w in downs])
    put["w_downB"] = np.stack([tiles(w[cut:], P) for w in downs])
    w = ev_w_in[0]
    half = CT * P
    conv = [np.concatenate([tiles(w[:, P * i:P * (i + 1)], P)[0], tiles(w[:, half + P * i:half + P * (i + 1)], P)[0]],
                           axis=1) for i in range(CT)]
    q_off = 2 * half
    query = [np.concatenate([w[:, q_off + HD * h:q_off + HD * (h + 1)] for h in (i, i + 4)], axis=1) for i in range(4)]
    kv = [w[:, q_off + half + P * i:q_off + half + P * (i + 1)] for i in range(2)]
    pairs = [(query[0], query[1]), (query[2], query[3]), (kv[0], kv[1])]
    put["w_ev_in"] = np.stack(conv + [np.concatenate([tiles(m, P)[0] for m in p], axis=1) for p in pairs])
    w = ev_w_out[0]
    rows = [w[:half]] + [w[half + HD * h:half + HD * (h + 1)] for i in range(4) for h in (i, i + 4)]
    w = np.concatenate(rows, axis=0)

    def two_wide(w):
        k, n = w.shape
        return w.reshape(k // P, P, n // (2 * P), 2, P).transpose(2, 1, 3, 0, 4).reshape(n // (2 * P), P, -1)

    put["w_ev_out"] = two_wide(w)
    w = od_w_in[0]
    put["w_od_in"] = np.concatenate([tiles(w[:, D * i:D * (i + 1)], DH) for i in (1, 2, 0, 3)], axis=0)
    put["w_od_gate"] = tiles(w[:, 4 * D:], 4 * HM)[0]
    put["w_od_out"] = two_wide(od_w_out[0])
    return {n: np.ascontiguousarray(a) for n, a in put.items()}


def kernel(**inputs):
    import concourse.bacc as bacc
    from concourse.bass_utils import run_bass_kernel_spmd

    nc = bacc.Bacc("TRN2", target_bir_lowering=False, num_devices=1)
    arrays = layout(**{n: np.asarray(a) for n, a in inputs.items()})
    t = {n: nc.dram_tensor(f"in_{n}", a.shape, mybir.dt.from_np(a.dtype), kind="ExternalInput").ap()
         for n, a in arrays.items()}
    out = nc.dram_tensor("out_y", (P, KT, LAT), F32, kind="ExternalOutput").ap()
    build(nc, t, out)
    r = run_bass_kernel_spmd(nc, [{f"in_{n}": a for n, a in arrays.items()}], core_ids=[0])
    y = r.results[0]["out_y"]
    return y.transpose(2, 1, 0).reshape(1, LAT, D)
```

```python
from contextlib import ExitStack

import numpy as np

import concourse.bass as bass
from concourse import mybir

P = 128
D = 1024
KT = D // P
LAT = 256
TOK = 2 * LAT
FF = 2816
FT = FF // P
PARTS = (12, 10)
EPS = 1e-6
CONV_W = 31
PAD = (CONV_W - 1) // 2
PADDED = LAT + 2 * PAD
CT = 4
HD = 64
NH_ATT = 8
KEYS = TOK
WINDOW = 128
HM = 4
DH = 256
GRID_W = 64
ROPE_FREQS = 16
NVEC = 9
JOBS = 2 * NVEC
UNIT = 2048
BIG = 1e30
F32 = mybir.dt.float32
F32R = mybir.dt.float32r
ALU = mybir.AluOpType
ACT = mybir.ActivationFunctionType
AX = mybir.AxisListType

COLS = {}
_at = 0
for _name, _n in (("ffn1", 16), ("mix", 16), ("ffn2", 16), ("final", 8), ("conv_b", 4), ("ln_g", 4), ("ln_b", 4),
                  ("norm_g", 8), ("conv_w", CONV_W * CT), ("mod_b", JOBS * KT), ("sink", NH_ATT), ("b_gate", 4 * HM)):
    COLS[_name] = (_at, _n)
    _at += _n
NCOL = _at

MATS = ("ident", "ones", "tri_up", "tri_low", "hide_after", "hide_before", "rot")
NMAT = len(MATS)


def schedule():
    base, size = {}, []

    def add(name, n, elements):
        base[name] = len(size)
        size.extend([elements] * n)

    def ffn(name):
        for part, n in zip("AB", PARTS):
            add(f"{name}up{part}", n, UNIT)
            add(f"{name}down{part}", KT, n * P)

    ffn("f0")
    add("ev_in", 7, UNIT)
    add("ev_out", 4, UNIT)
    ffn("f1")
    ffn("f2")
    add("od_gate", 1, KT * 4 * HM)
    add("od_in", 16, UNIT)
    add("od_out", 4, UNIT)
    ffn("f3")
    return base, size


def build(nc, t, out):
    U, SIZE = schedule()
    NU = len(SIZE)
    with ExitStack() as ctx:
        def sb(name, shape, dt=F32, scope=ctx):
            return scope.enter_context(nc.sbuf_tensor(name, shape, dt))

        def sem(name):
            return ctx.enter_context(nc.semaphore(name))

        xT = sb("xT", [P, KT, TOK])
        hn_hi = sb("hn_hi", [P, KT, TOK], F32R)
        hn_lo = sb("hn_lo", [P, KT, TOK], F32R)
        raw = sb("raw", [P, 2, UNIT])
        w_hi = sb("w_hi", [P, 2, UNIT], F32R)
        w_lo = sb("w_lo", [P, 2, UNIT], F32R)
        gact = sb("gact", [P, 2, TOK])
        prod = sb("prod", [P, 2, TOK])
        t_ring = sb("t_ring", [P, 2, TOK])
        sq = sb("sq", [P, 2, TOK])
        acc = sb("acc", [P, TOK])
        sd = sb("sd", [P, TOK])
        rstd = sb("rstd", [P, TOK])
        inv = sb("inv", [P, 2, 4])
        eps = sb("eps", [P, 1])
        mats = sb("mats", [P, NMAT, P])
        cols = sb("cols", [P, NCOL])
        sel = sb("sel", [P, 8])
        shared = sb("shared", [P, 2 * LAT])
        mrow = shared[:, 0:LAT]
        c_in = mrow
        c_act = shared[:, LAT:2 * LAT].rearrange("p (k c) -> p k c", k=KT)
        modT = sb("modT", [P, JOBS, KT, 2])
        mat = {n: mats[:, i, :] for i, n in enumerate(MATS)}
        ident, ones = mat["ident"], mat["ones"]

        with ExitStack() as s:
            a_hi = sb("a_hi", [P, PARTS[0], TOK], F32R, s)
            a_lo = sb("a_lo", [P, PARTS[0], TOK], F32R, s)
            mod_raw = sb("mod_raw", [P, KT, D], F32, s)
        with ExitStack() as s:
            mod_raw1 = sb("mod_raw1", [P, KT, D], F32, s)
        with ExitStack() as s:
            upad = sb("upad", [P, CT, 2, PADDED], F32, s)
            y = sb("y", [P, CT, TOK], F32, s)
            qk = sb("qk", [P, CT + 1, TOK], F32, s)
            v_att = sb("v_att", [P, 4, P], F32, s)
            cos_sin = sb("cos_sin", [P, 2, LAT], F32, s)
            att_mask = sb("att_mask", [P, 2, KEYS], F32, s)
            pT = sb("pT", [P, 2, 4, LAT], F32, s)
            att_cols = sb("att_cols", [P, 6, 32], F32, s)
        with ExitStack() as s:
            k_tok = sb("k_tok", [P, 4, HM, DH], F32, s)
            v_tok = sb("v_tok", [P, 4, HM, DH + 1], F32, s)
            qT = sb("qT", [P, KT, LAT], F32, s)
            kT = sb("kT", [P, KT, LAT], F32, s)
            oT = sb("oT", [P, KT, LAT], F32, s)
            state = sb("state", [P, 2, HM, 2, DH + 1], F32, s)
            decayed = sb("decayed", [P, 2, 2, HM, P], F32, s)
            out_cols = sb("out_cols", [P, 2, 16], F32, s)
            ms_cols = sb("ms_cols", [P, 2, 8], F32, s)
        gates = shared[:].rearrange("p (n d s h) -> p n d s h", d=2, s=4, h=HM)
        GATE = {n: gates[:, i] for i, n in enumerate(
            ("li", "f", "abs", "exp", "ln", "lf", "b", "end", "a", "amax", "cmax", "m", "mm", "mq", "arg", "val"))}

        ps = ctx.enter_context(nc.psum_tensor("ps", [P, 8, TOK], F32))

        unit_in = [sem("unit_in0"), sem("unit_in1")]
        hi_made = sem("hi_made")
        lo_made = sem("lo_made")
        unit_mm = sem("unit_mm")
        unit_evac = sem("unit_evac")
        gate_made = sem("gate_made")
        a_hi_made = sem("a_hi_made")
        a_made = sem("a_made")
        x_in = sem("x_in")
        sq_made = sem("sq_made")
        sq_added = sem("sq_added")
        acc_clear = sem("acc_clear")
        norm_mm = sem("norm_mm")
        sd_made = sem("sd_made")
        rstd_made = sem("rstd_made")
        rstd_mm = sem("rstd_mm")
        t_made = sem("t_made")
        hn_hi_made = sem("hn_hi_made")
        hn_made = sem("hn_made")
        par_in = sem("par_in")
        c_made = sem("c_made")
        mod_first = sem("mod_first")
        mod_second = [sem(f"mod_second{i}") for i in range(4)]
        mod_in = sem("mod_in")
        mod_mm = sem("mod_mm")
        mod_row = sem("mod_row")
        mod_tr = sem("mod_tr")
        mod_made = sem("mod_made")
        link_v = sem("link_v")
        link_s = sem("link_s")
        ev_in = sem("ev_in")
        tap_done = sem("tap_done")
        pad_clear = sem("pad_clear")
        qk_raw = sem("qk_raw")
        v_rows = sem("v_rows")
        v_mm = sem("v_mm")
        v_made = sem("v_made")
        rot_mm = sem("rot_mm")
        turned_one = sem("turned_one")
        roped = sem("roped")
        ln_mm = sem("ln_mm")
        ln_cent = sem("ln_cent")
        ln_sq = sem("ln_sq")
        ln_sd = sem("ln_sd")
        ln_t = sem("ln_t")
        ln_hi = sem("ln_hi")
        mix_made = sem("mix_made")
        s_mm = sem("s_mm")
        max_made = sem("max_made")
        exp_made = sem("exp_made")
        den_made = sem("den_made")
        p_made = sem("p_made")
        pT_mm = sem("pT_mm")
        pT_made = sem("pT_made")
        pv_mm = sem("pv_mm")
        att_hi = sem("att_hi")
        gate_rows = sem("gate_rows")
        gates_mm = sem("gates_mm")
        gates_in = sem("gates_in")
        ln1p = sem("ln1p")
        lf_made = sem("lf_made")
        cum_mm = sem("cum_mm")
        diag_made = sem("diag_made")
        diag_mm = sem("diag_mm")
        arg_made = sem("arg_made")
        val_made = sem("val_made")
        hid_made = sem("hid_made")
        dec_made = sem("dec_made")
        kT_mm = sem("kT_mm")
        kT_made = sem("kT_made")
        st_mm = sem("st_mm")
        sT_made = sem("sT_made")
        wk_made = sem("wk_made")
        st_up = sem("st_up")
        st_made = sem("st_made")
        out_mm = sem("out_mm")
        out_scaled = sem("out_scaled")
        out_made = sem("out_made")
        h_made = sem("h_made")
        ss_made = sem("ss_made")
        hsd_made = sem("hsd_made")
        hnorm = sem("hnorm")
        hT_mm = sem("hT_mm")
        hz_made = sem("hz_made")
        hz_hi = sem("hz_hi")
        y_made = sem("y_made")
        y_out = [sem("y_out0"), sem("y_out1")]

        CONV_G = FT
        GBASE = {"f0": 0, "f1": FT + CT, "f2": 2 * FT + CT, "f3": 3 * FT + CT}
        ABASE = {"f0": 0, "f1": FT, "f2": 2 * FT, "f3": 3 * FT}
        OD_G = GBASE["f3"]
        GBASE["f3"] += 4
        W = [TOK] * 5 + [LAT] * 2
        GAIN = [("ffn1", 0), ("mix", 0), ("ffn2", 0), ("ffn1", KT), ("mix", KT), ("ffn2", KT), ("final", 0)]
        JOB_OF = {"f0A": (2, 6), "f0B": (8, 5)}
        NORM_JOB = {1: 13, 2: 14, 3: 16}
        TURN_JOB = {"f1A": 15}
        KEY_JOB = 17

        def column_bank(m):
            return bank(U["od_gate"], 1) if isinstance(m, int) and m == KEY_JOB else 5


        def bank(u, j=0):
            return 2 * (u % 2) + j

        KEY_BANKS = (bank(U["od_in"]), bank(U["od_in"], 1), 5, 6)

        def col(name, i, n=1):
            return cols[:, COLS[name][0] + i:COLS[name][0] + i + n]

        def streams(w):
            return range(w // LAT)

        def tokens(s):
            return slice(s * LAT, (s + 1) * LAT)

        def pairs(eng, n, body, first=False):
            lo = 1 if first else 0
            if first:
                body(0, False)
            if n - 1 > lo:
                with eng.Fori(lo, n - 1) as r:
                    body(r, False)
            body(n - 1, True)

        STEP_TILE = ((2, 3, 0, 1), (3, 2, 1, 0))
        TAPS = 2 * CONV_W
        EARLY = 28

        def taps_by(j):
            if j < 9:
                return EARLY + (TAPS - EARLY) * (j + 1 if j < 4 else j) // 8
            return min(2 * TAPS, TAPS + TAPS * (j - 9) // 24)

        ATT = [(tt, s, h2, qt) for tt in range(4) for s in range(2) for h2 in range(2) for qt in range(2)]
        OUTS = [(2, d, h) for d in range(2) for h in range(HM)] + [(3, d, h) for d in range(2) for h in range(HM)]
        STATES = [(s, d, h) for s in range(3) for d in range(2) for h in range(HM)]

        block = ctx.enter_context(nc.Block())

        @block.sync
        def _(sp):
            def load(u0, j, r, src, n):
                u = u0 + j + 2 * r
                if isinstance(r, int) and u < 2:
                    pass
                else:
                    sp.wait_ge(lo_made, u - 1)
                sp.dma_start(raw[:, (u0 + j) % 2, 0:n], src).then_inc(unit_in[(u0 + j) % 2], 16)

            sp.dma_start(c_in, t["c_in"]).then_inc(par_in, 16)
            sp.dma_start(sel[:], t["sel"]).then_inc(par_in, 16)
            sp.dma_start(mats[:], t["mats"]).then_inc(par_in, 16)
            sp.dma_start(mod_raw[:], t["mod_w"][0]).then_inc(mod_first, 16)
            sp.dma_start(cols[:], t["cols"]).then_inc(par_in, 16)
            sp.dma_start(xT[:], t["xT"]).then_inc(x_in, 16)
            load(U["f0upA"], 0, 0, t["w_up"][0, 0], UNIT)
            for i in range(4):
                sp.dma_start(mod_raw1[:, 2 * i:2 * i + 2], t["mod_w"][1][:, 2 * i:2 * i + 2]).then_inc(mod_second[i], 16)

            def ffn(f, name):
                at = 0
                for part, n in zip("AB", PARTS):
                    if name == "f0" and part == "A":
                        load(U["f0upA"], 1, 0, t["w_up"][f, 1], UNIT)
                        first = 1
                    else:
                        first = 0
                    with sp.Fori(first, n // 2) as r:
                        for j in range(2):
                            load(U[f"{name}up{part}"], j, r, t["w_up"][f, at + 2 * r + j], UNIT)
                    with sp.Fori(0, KT // 2) as r:
                        for j in range(2):
                            load(U[f"{name}down{part}"], j, r, t[f"w_down{part}"][f, 2 * r + j], n * P)
                    at += n

            ffn(0, "f0")
            for i in range(2):
                load(U["ev_in"] + i, 0, 0, t["w_ev_in"][i], UNIT)
            sp.wait_ge(unit_mm, U["ev_in"])
            sp.dma_start(cos_sin[:], t["cos_sin"]).then_inc(ev_in, 16)
            sp.dma_start(att_mask[:], t["att_mask"]).then_inc(ev_in, 16)
            for i in range(2, 7):
                load(U["ev_in"] + i, 0, 0, t["w_ev_in"][i], UNIT)
            for i in range(4):
                load(U["ev_out"] + i, 0, 0, t["w_ev_out"][i], UNIT)
            ffn(1, "f1")
            ffn(2, "f2")
            load(U["od_gate"], 0, 0, t["w_od_gate"], KT * 4 * HM)
            for i in range(16):
                load(U["od_in"] + i, 0, 0, t["w_od_in"][i], UNIT)
            for i in range(4):
                load(U["od_out"] + i, 0, 0, t["w_od_out"][i], UNIT)
            ffn(3, "f3")
            for k in range(KT):
                sp.wait_ge(y_made, k + 1)
                sp.dma_start(out[:, k, :], t_ring[:, k % 2, 0:LAT]).then_inc(y_out[k % 2], 16)
            for i in range(2):
                sp.wait_ge(y_out[i], 16 * KT // 2)

        @block.gpsimd
        def _(pool):
            pool.wait_ge(mod_mm, 1)
            pool.dma_start(mod_raw[:], t["mod_w"][2]).then_inc(mod_in, 16)
            with pool.Fori(3, JOBS) as m:
                pool.wait_ge(mod_mm, m)
                pool.dma_start(mod_raw[:], t["mod_w"][m]).then_inc(mod_in, 16)

        @block.tensor
        def _(pe):
            def three(o, lhs, rhs, first, last):
                (lh, ll), (rh, rl) = lhs, rhs
                pe.matmul(o, lh, rh, start=first, stop=False)
                pe.matmul(o, lh, rl, start=False, stop=False)
                return pe.matmul(o, ll, rh, start=False, stop=last)

            def weights(u0, a, b):
                return w_hi[:, u0 % 2, a:b], w_lo[:, u0 % 2, a:b]

            def begin(u, static=True):
                pe.wait_ge(lo_made, u + 1)
                if not static or u >= 2:
                    pe.wait_ge(unit_evac, u - 1)

            def unit(u0, r, nb, nk, w, operand, at, ready=None):
                begin(u0 + 2 * r, isinstance(r, int))
                for k in range(nk):
                    if ready:
                        ready(k)
                    for b in range(nb):
                        last = three(ps[:, bank(u0, b), 0:w], weights(u0, at(b, k), at(b, k) + P),
                                     (operand[0][:, k, 0:w], operand[1][:, k, 0:w]), k == 0, k == nk - 1)
                last.then_inc(unit_mm, 1)

            def mod_products(m, static, k0=0, k1=KT):
                if static and m == 0:
                    pe.wait_ge(mod_first, 16)
                elif k0 == 0 and (not static or m > 1):
                    pe.wait_ge(mod_in, 16 * m - 16)
                source = mod_raw1 if static and m == 1 else mod_raw
                if k0 == 0 and (not static or m > 0):
                    pe.wait_ge(mod_row, m)
                for k in range(k0, k1):
                    if static and m == 1 and k % 2 == 0:
                        pe.wait_ge(mod_second[k // 2], 16)
                    for g in range(4):
                        last = pe.matmul(ps[32 * g:32 * g + 32, 4, 0:LAT], c_act[:, k, :],
                                         source[:, k, g * LAT:(g + 1) * LAT], start=(k == 0), stop=(k == KT - 1))
                if k1 == KT:
                    last.then_inc(mod_mm, 1)

            def mod_columns(m, static):
                pe.wait_ge(mod_row, m + 1)
                if not static or m > 0:
                    pe.wait_ge(mod_made, m)
                for b in range(2):
                    last = pe.matmul(ps[:, column_bank(m), 8 * b:8 * b + 8], mrow[:, b * P:(b + 1) * P], sel[:],
                                     start=True, stop=True)
                last.then_inc(mod_tr, 1)

            def norm(n):
                job = NORM_JOB.get(n)
                if job:
                    mod_products(job, True, 0, 4)
                pe.wait_ge(sq_added, KT * (n + 1))
                for i in range(W[n] // P):
                    last = pe.matmul(ps[:, 6, i:i + 1], acc[:, i * P:(i + 1) * P], ones[:, 0:1], start=True, stop=True)
                last.then_inc(norm_mm, 1)
                if job:
                    mod_products(job, True, 4, 6)
                pe.wait_ge(rstd_made, n + 1)
                pe.matmul(ps[:, 7, 0:W[n]], ones, rstd[:, 0:W[n]], start=True, stop=True).then_inc(rstd_mm, 1)
                if job:
                    mod_products(job, True, 6, KT)

            def hn_ready(n):
                def ready(k):
                    pe.wait_ge(hn_made, KT * n + k + 1)
                    if k == 5 and n in NORM_JOB:
                        mod_columns(NORM_JOB[n], True)
                return ready

            def ffn(name, f, n, w):
                done = ABASE[name]
                for part, nf in zip("AB", PARTS):
                    up, down = U[f"{name}up{part}"], U[f"{name}down{part}"]
                    job, carry = JOB_OF.get(name + part, (0, 0))

                    def pair(r, end):
                        has = carry and (carry == nf // 2 or not end)
                        m = job + r
                        for j in range(2):
                            unit(up + j, r, 2, KT, w, (hn_hi, hn_lo), lambda b, k: b * KT * P + k * P,
                                 hn_ready(n) if isinstance(r, int) and r == 0 and j == 0 and part == "A" else None)
                            if has and j == 0:
                                mod_products(m, False)
                            if has and j == 1:
                                mod_columns(m, False)

                    pairs(pe, nf // 2, pair, True)
                    done += nf
                    if name + part in TURN_JOB:
                        mod_products(TURN_JOB[name + part], True)
                        mod_columns(TURN_JOB[name + part], True)

                    def down_pair(r, end):
                        for j in range(2):
                            ready = None
                            if isinstance(r, int) and r == 0 and j == 0:
                                ready = lambda k: pe.wait_ge(a_made, done - nf + k + 1)
                            unit(down + j, r, 1, nf, w, (a_hi, a_lo), lambda b, k: k * P, ready)

                    pairs(pe, KT // 2, down_pair, True)

            pe.wait_ge(par_in, 64)
            pe.wait_ge(c_made, 1)
            mod_products(0, True)
            mod_columns(0, True)
            norm(0)
            mod_products(1, True)
            mod_columns(1, True)
            ffn("f0", 0, 0, TOK)
            norm(1)

            E = U["ev_in"]

            def two(b, k):
                return b * KT * P + k * P

            for c in range(2):
                unit(E + c, 0, 2, KT, TOK, (hn_hi, hn_lo), two, hn_ready(1) if c == 0 else None)

            def rotate(i):
                pe.wait_ge(qk_raw, i + 1)
                if i >= 2:
                    pe.wait_ge(roped, i - 1)
                pe.matmul(ps[:, 6 + i % 2, 0:LAT], mat["rot"], qk[:, i, 0:LAT],
                          start=True, stop=True).then_inc(rot_mm, 1)

            unit(E + 2, 0, 2, KT, TOK, (hn_hi, hn_lo), two)
            unit(E + 3, 0, 2, KT, TOK, (hn_hi, hn_lo), two)
            rotate(0)
            rotate(1)
            unit(E + 4, 0, 2, KT, TOK, (hn_hi, hn_lo), two)

            def conv_step(c, n):
                k = n if c == 2 else (n + CT) % KT
                u = E + 3 + c
                if n == 0:
                    pe.wait_ge(lo_made, u + 1)
                    pe.wait_ge(unit_evac, E + 4 if c == 2 else u)
                for b in range(2):
                    last = three(ps[:, 2 + b, :], weights(u, two(b, k), two(b, k) + P),
                                 (hn_hi[:, k, :], hn_lo[:, k, :]), n == 0, n == KT - 1)
                if n == KT - 1:
                    last.then_inc(unit_mm, 1)

            rotate(2)
            rotate(3)
            conv_step(2, 0)
            conv_step(2, 1)
            pe.wait_ge(v_rows, 1)
            for i in range(4):
                last = pe.transpose(ps[:, 5, i * P:(i + 1) * P], gact[:, 0, i * P:(i + 1) * P], ident)
            last.then_inc(v_mm, 1)
            rotate(4)
            conv_step(2, 2)
            conv_step(2, 3)

            pe.wait_ge(roped, 5)
            pe.wait_ge(v_made, 1)

            def scores(j):
                tt, s, h2, qt = ATT[j]
                if j >= 2:
                    pe.wait_ge(exp_made, j - 1)
                k0 = LAT * s
                a = LAT * s + qt * P
                pe.matmul(ps[:, 4 + j % 2, k0:KEYS], qk[64 * h2:64 * h2 + 64, tt, a:a + P],
                          qk[64 * h2:64 * h2 + 64, CT, k0:KEYS], start=True, stop=True).then_inc(s_mm, 1)

            def turn(j):
                tt, s, h2, qt = ATT[j]
                pe.wait_ge(p_made, j + 1)
                if j >= 2:
                    pe.wait_ge(pT_made, j - 1)
                for kt in range(2 * s, 4):
                    last = pe.transpose(ps[:, 6 + j % 2, kt * P:(kt + 1) * P], prod[:, j % 2, kt * P:(kt + 1) * P],
                                        ident)
                last.then_inc(pT_mm, 1)

            def values(j, half):
                tt, s, h2, qt = ATT[j]
                g = j // 4
                kts = range(2 * s, 4)
                kts = kts[:len(kts) // 2] if half == 0 else kts[len(kts) // 2:]
                if half == 0:
                    pe.wait_ge(pT_made, j + 1)
                    if g >= 2:
                        pe.wait_ge(mix_made, g - 1)
                    if g == 0:
                        pe.wait_ge(unit_evac, E + 5)
                for kt in kts:
                    last = pe.matmul(ps[64 * h2:64 * h2 + 64, g % 2, 0:LAT], v_att[:, kt, 64 * h2:64 * h2 + 64],
                                     pT[:, (j // 2) % 2, kt, :], start=(kt == 2 * s), stop=(kt == 3))
                if half == 1:
                    last.then_inc(pv_mm, 1)

            NJ = len(ATT)
            scores(0)
            for j in range(NJ + 3):
                if j + 1 < NJ:
                    scores(j + 1)
                if j < 4:
                    conv_step(2, 4 + j)
                if 5 <= j < 9:
                    conv_step(3, 2 * j - 10)
                    conv_step(3, 2 * j - 9)
                if 1 <= j < NJ + 1:
                    turn(j - 1)
                if j >= 3:
                    values(j - 2 - (j + 1) % 2, (j + 1) % 2)

            pe.wait_ge(pT_made, NJ)
            for c in range(CT):
                pe.wait_ge(tap_done, TAPS * (c // 2) + TAPS - 1 + c % 2)
                last = pe.matmul(ps[:, 7, :], ones, y[:, c, :], start=(c == 0), stop=(c == CT - 1))
            last.then_inc(ln_mm, 1)

            pe.wait_ge(unit_evac, U["ev_out"])
            for i in range(2):
                u = U["ev_out"] + i
                pe.wait_ge(lo_made, u + 1)
                for k in range(CT, KT):
                    pe.wait_ge(mix_made, 2 * (k - CT) + 2)
                    for b in range(2):
                        three(ps[:, bank(u, b), :], weights(u, two(b, k), two(b, k) + P),
                              (hn_hi[:, k, :], hn_lo[:, k, :]), k == CT, False)
                if i == 0:
                    for c in range(CT):
                        pe.wait_ge(ln_sq, c + 1)
                        pe.matmul(ps[:, 6, :], ones, sq[:, c % 2, :], start=(c == 0), stop=(c == CT - 1))\
                            .then_inc(ln_mm, 1)
            for i in range(2):
                u = U["ev_out"] + i
                for k in range(CT):
                    if i == 0:
                        pe.wait_ge(mix_made, 8 + k + 1)
                    for b in range(2):
                        last = three(ps[:, bank(u, b), :], weights(u, two(b, k), two(b, k) + P),
                                     (hn_hi[:, k, :], hn_lo[:, k, :]), False, k == CT - 1)
                last.then_inc(unit_mm, 1)

            for i in range(2, 4):
                unit(U["ev_out"] + i, 0, 2, KT, TOK, (hn_hi, hn_lo), two)
            norm(2)
            ffn("f1", 1, 2, TOK)
            norm(3)
            ffn("f2", 2, 3, TOK)
            norm(4)

            u = U["od_gate"]
            begin(u + 1)
            for k in range(KT):
                pe.wait_ge(hn_made, KT * 4 + k + 1)
                mod_products(KEY_JOB, True, k, k + 1)
                three(ps[0:16, bank(u), :], weights(u, k * 16, (k + 1) * 16), (hn_hi[:, k, :], hn_lo[:, k, :]),
                      k == 0, k == KT - 1)
                for i in range(4):
                    last = three(ps[:, KEY_BANKS[i], 0:DH],
                                 (hn_hi[:, k, i * P:(i + 1) * P], hn_lo[:, k, i * P:(i + 1) * P]),
                                 weights(u + 1, k * DH, (k + 1) * DH), k == 0, k == KT - 1)
            last.then_inc(unit_mm, 2)
            mod_columns(KEY_JOB, True)
            pe.wait_ge(gate_rows, 1)
            for i in range(4):
                last = pe.transpose(ps[:, bank(u), i * 16:(i + 1) * 16], gact[0:16, 0, i * P:(i + 1) * P],
                                    ident[0:16, 0:16])
            last.then_inc(gates_mm, 1)
            for n in range(8):
                u = U["od_in"] + n
                if n > 0:
                    begin(u)
                    for i in range(4):
                        for k in range(KT):
                            last = three(ps[:, bank(u, i // 2), (i % 2) * DH:(i % 2 + 1) * DH],
                                         (hn_hi[:, k, i * P:(i + 1) * P], hn_lo[:, k, i * P:(i + 1) * P]),
                                         weights(u, k * DH, (k + 1) * DH), k == 0, k == KT - 1)
                    last.then_inc(unit_mm, 1)
                if n == 1:
                    pe.wait_ge(lf_made, 1)
                    lf = GATE["lf"].rearrange("p d s h -> p d (s h)")
                    pe.matmul(ps[:, 7, 0:16], mat["tri_up"], lf[:, 0, :], start=True, stop=True)
                    pe.matmul(ps[:, 7, 16:32], mat["tri_low"], lf[:, 1, :], start=True, stop=True)
                    pe.matmul(ps[:, 7, 32:64], ones, lf.rearrange("p d n -> p (d n)"), start=True, stop=True)\
                        .then_inc(cum_mm, 1)
                if 2 <= n <= 7:
                    for i in range(2 * n - 4, 2 * n - 2):
                        pe.wait_ge(diag_made, i + 1)
                        pe.matmul(ps[:, 4 + i % 2, :], ones, sq[:, i % 2, :], start=True, stop=True).then_inc(diag_mm, 1)
            for n in range(8):
                unit(U["od_in"] + 8 + n, 0, 2, KT, LAT, (hn_hi, hn_lo), lambda b, k: k * DH + b * P)

            pe.wait_ge(hid_made, 4)
            for h in range(HM):
                pe.wait_ge(unit_evac, U["od_in"] + h + 1)
                if h >= 2:
                    pe.wait_ge(kT_made, h - 1)
                for kt in range(2):
                    for i in range(2):
                        last = pe.transpose(ps[:, 6 + h % 2, (2 * kt + i) * P:(2 * kt + i + 1) * P],
                                            k_tok[:, i, h, kt * P:(kt + 1) * P], ident)
                last.then_inc(kT_mm, 1)
            pe.wait_ge(unit_evac, U["od_in"] + 12)
            for i in range(2):
                for h in range(HM):
                    pe.wait_ge(kT_made, h + 1)
                    for kt in range(2):
                        last = pe.matmul(ps[:, 4 + i, h * P:(h + 1) * P], kT[:, 2 * h + kt, i * P:(i + 1) * P],
                                         qT[:, 2 * h + kt, i * P:(i + 1) * P], start=(kt == 0), stop=(kt == 1))
                last.then_inc(st_mm, 1)

            pe.wait_ge(unit_evac, U["od_out"])

            def state_up(n):
                s, d, h = STATES[n]
                pe.wait_ge(wk_made, n + 1)
                if n >= 2:
                    pe.wait_ge(st_made, n - 1)
                for kt in range(2):
                    last = pe.matmul(ps[:, 2 * (n % 2) + kt, 0:DH + 1], t_ring[:, n % 2, kt * P:(kt + 1) * P],
                                     v_tok[:, STEP_TILE[d][s], h, :], start=True, stop=True)
                last.then_inc(st_up, 1)

            def outputs(n):
                s, d, h = OUTS[n]
                i = STEP_TILE[d][s]
                if n == 0:
                    pe.wait_ge(sT_made, 4)
                if n >= 2:
                    pe.wait_ge(out_made, n - 1)
                pe.wait_ge(st_made, 8 * (s - 1) + HM * d + h + 1)
                pe.matmul(ps[:, 6 + n % 2, 0:DH + 1], decayed[:, s - 2, d, h, :], v_tok[:, i, h, :],
                          start=True, stop=True)
                for kt in range(2):
                    last = pe.matmul(ps[:, 4 + n % 2, 0:DH + 1], qT[:, 2 * h + kt, i * P:(i + 1) * P],
                                     state[:, d, h, kt, :], start=(kt == 0), stop=(kt == 1))
                last.then_inc(out_mm, 1)

            for n in range(16):
                state_up(n)
            for n in range(8):
                outputs(n)
            for n in range(8):
                state_up(16 + n)
            for n in range(8):
                outputs(8 + n)

            for h in range(HM):
                pe.wait_ge(hnorm, 2 * h + 2)
                if h >= 2:
                    pe.wait_ge(hz_made, h - 1)
                for kt in range(2):
                    for i in range(2):
                        last = pe.transpose(ps[:, 6 + h % 2, (2 * kt + i) * P:(2 * kt + i + 1) * P],
                                            xT[:, i * HM + h, LAT + kt * P:LAT + (kt + 1) * P], ident)
                last.then_inc(hT_mm, 1)
            for i in range(4):
                def ready(k):
                    pe.wait_ge(mix_made, CT + 8 + k // 2 + 1)
                unit(U["od_out"] + i, 0, 2, KT, LAT, (hn_hi, hn_lo), two, ready if i == 0 else None)
            norm(5)
            ffn("f3", 3, 5, LAT)
            norm(6)

        @block.scalar
        def _(act):
            linked = [0]

            def link(ins):
                linked[0] += 1
                ins.then_inc(link_s, 1)
                act.wait_ge(link_s, linked[0])

            def head(u0, r, n):
                u = u0 + 2 * r
                act.wait_ge(unit_in[u0 % 2], 16 * (u0 // 2 + 1) + 16 * r)
                if not (isinstance(r, int) and u < 2):
                    act.wait_ge(unit_mm, u - 1)
                act.activation(w_hi[:, u0 % 2, 0:n], raw[:, u0 % 2, 0:n], ACT.Copy).then_inc(hi_made, 1)

            def head_of(u):
                if u < NU:
                    head(u, 0, SIZE[u])

            def norm_root(n):
                w = W[n]
                act.preload_act_table(ACT.Sqrt)
                act.wait_ge(norm_mm, n + 1)
                act.activation(inv[:, 0, 0:w // P], ps[:, 6, 0:w // P], ACT.Sqrt, bias=eps[:], scale=1.0 / D)\
                    .then_inc(sd_made, 1)

            def norm_heads(n):
                w = W[n]
                for k in range(KT):
                    act.wait_ge(t_made, KT * n + k + 1)
                    for s in streams(w):
                        last = act.activation(hn_hi[:, k, tokens(s)], t_ring[:, k % 2, tokens(s)], ACT.Identity,
                                              bias=modT[:, 3 * n, k, s:s + 1])
                    last.then_inc(hn_hi_made, 1)
                    if k == 2 and n in NORM_JOB:
                        mod_rows(NORM_JOB[n], True)

            def norm(n):
                norm_root(n)
                if n < 6:
                    norm_heads(n)

            def mod_rows(m, static):
                act.wait_ge(mod_mm, m + 1)
                if not static or m > 0:
                    act.wait_ge(mod_tr, m)
                act.activation(mrow, ps[:, 4, 0:LAT], ACT.Copy).then_inc(mod_row, 1)

            def square_tile(n, u, d0, r, w):
                act.wait_ge(unit_evac, u + 1)
                act.wait_ge(sq_added, KT * n + d0 + 2 * r - 1)
                act.activation(sq[:, d0 % 2, 0:w], xT[:, d0 + 2 * r, 0:w], ACT.Square).then_inc(sq_made, 1)

            def ffn(name, f, n, w):
                tile = 0
                for part, nf in zip("AB", PARTS):
                    up, down = U[f"{name}up{part}"], U[f"{name}down{part}"]
                    job, carry = JOB_OF.get(name + part, (0, 0))
                    a0 = ABASE[name] + tile

                    def pair(r, end):
                        has = carry and (carry == nf // 2 or not end)
                        for j in range(2):
                            if end:
                                head_of(up + j + 2 * r + 2)
                            else:
                                head(up + j + 2, r, UNIT)
                            act.wait_ge(unit_mm, up + j + 2 * r + 1)
                            act.activation(gact[:, j, 0:w], ps[:, bank(up + j, 0), 0:w], ACT.Silu).then_inc(gate_made, 1)
                            act.wait_ge(unit_evac, up + j + 2 * r + 1)
                            act.activation(a_hi[:, j + 2 * r, 0:w], prod[:, j, 0:w], ACT.Copy).then_inc(a_hi_made, 1)
                            if has and j == 0:
                                mod_rows(job + r, False)

                    act.preload_act_table(ACT.Silu)
                    pairs(act, nf // 2, pair)
                    tile += nf
                    if name + part in TURN_JOB:
                        mod_rows(TURN_JOB[name + part], True)

                    def down_pair(r, end):
                        for j in range(2):
                            if end:
                                head_of(down + j + 2 * r + 2)
                            else:
                                head(down + j + 2, r, nf * P)
                            if part == "B":
                                square_tile(n + 1, down + j + 2 * r, j, r, w)

                    pairs(act, KT // 2, down_pair, part == "B")

            act.wait_ge(par_in, 64)
            act.activation(shared[:, LAT:2 * LAT], c_in, ACT.Silu).then_inc(c_made, 1)
            act.wait_ge(x_in, 16)
            for d in range(KT):
                if d >= 2:
                    act.wait_ge(sq_added, d - 1)
                act.activation(sq[:, d % 2, :], xT[:, d, :], ACT.Square).then_inc(sq_made, 1)
            mod_rows(0, True)
            norm_root(0)
            head_of(0)
            mod_rows(1, True)
            norm_heads(0)
            head_of(1)
            ffn("f0", 0, 0, TOK)
            norm(1)

            E = U["ev_in"]
            for c in range(2):
                head_of(E + c + 2)
                act.wait_ge(unit_mm, E + c + 1)
                act.activation(gact[:, c % 2, :], ps[:, bank(E + c, 1), :], ACT.Sigmoid).then_inc(gate_made, 1)
            for n in range(2):
                head_of(E + 4 + n)
                act.wait_ge(unit_mm, E + 3 + n)
                for b in range(2):
                    act.activation(qk[:, 2 * n + b, :], ps[:, bank(E + 2 + n, b), :], ACT.Copy).then_inc(qk_raw, 1)
            act.wait_ge(unit_mm, E + 5)
            act.activation(qk[:, CT, :], ps[:, bank(E + 4), :], ACT.Copy).then_inc(qk_raw, 1)
            act.activation(gact[:, 0, :], ps[:, bank(E + 4, 1), :], ACT.Copy).then_inc(v_rows, 1)
            head_of(E + 6)
            act.wait_ge(v_mm, 1)
            act.activation(v_att[:].rearrange("p a b -> p (a b)"), ps[:, 5, :], ACT.Copy).then_inc(v_made, 1)

            def expo(j):
                tt, s, h2, qt = ATT[j]
                act.wait_ge(max_made, j + 1)
                if j >= 2:
                    act.wait_ge(pT_mm, j - 1)
                src = ps[:, 4 + j % 2, LAT:KEYS] if s else gact[:, j % 2, :]
                neg = att_cols[:, 1, j:j + 1]
                act.activation(prod[:, j % 2, LAT * s:KEYS], src, ACT.Exp, bias=neg, scale=HD ** -0.5,
                               accum_out=att_cols[:, 2, j:j + 1])
                act.activation(att_cols[:, 3, j:j + 1], col("sink", tt + 4 * h2), ACT.Exp, bias=neg).then_inc(exp_made, 1)

            def normalise(j):
                tt, s, h2, qt = ATT[j]
                act.wait_ge(den_made, j + 1)
                p = prod[:, j % 2, LAT * s:KEYS]
                act.activation(p, p, ACT.Copy, scale=att_cols[:, 5, j:j + 1]).then_inc(p_made, 1)

            def turned(j):
                tt, s, h2, qt = ATT[j]
                act.wait_ge(pT_mm, j + 1)
                if j // 2 >= 2:
                    act.wait_ge(pv_mm, j // 2 - 1)
                act.activation(pT[:, (j // 2) % 2, 2 * s:4, qt * P:(qt + 1) * P],
                               ps[:, 6 + j % 2, 2 * s * P:4 * P].rearrange("p (k q) -> p k q", q=P),
                               ACT.Copy).then_inc(pT_made, 1)

            def att_head(g):
                act.wait_ge(pv_mm, 2 * g + 2)
                act.activation(hn_hi[:, CT + g // 2, tokens(g % 2)], ps[:, g % 2, 0:LAT], ACT.Copy).then_inc(att_hi, 1)

            NJ = len(ATT)
            for j in range(NJ + 3):
                if j < NJ:
                    expo(j)
                if 1 <= j < NJ + 1:
                    normalise(j - 1)
                if 2 <= j < NJ + 2:
                    turned(j - 2)
                if j in (4, 9):
                    c = 2 if j == 4 else 3
                    act.wait_ge(unit_mm, E + 4 + c)
                    act.activation(t_ring[:, c % 2, :], ps[:, 3, :], ACT.Sigmoid).then_inc(gate_made, 1)
                    head_of(E + 5 + c)
                if j >= 6 and (j - 2) % 4 == 0:
                    att_head((j - 6) // 4)
            for c in range(CT):
                act.wait_ge(ln_cent, c + 1)
                if c >= 2:
                    act.wait_ge(ln_mm, c)
                act.activation(sq[:, c % 2, :], y[:, c, :], ACT.Square).then_inc(ln_sq, 1)
            act.wait_ge(ln_mm, 1 + CT)
            act.activation(sd[:], ps[:, 6, :], ACT.Sqrt, bias=eps[:], scale=1.0 / (CT * P)).then_inc(ln_sd, 1)
            for c in range(CT):
                act.wait_ge(ln_t, c + 1)
                link(act.activation(gact[:, c % 2, :], t_ring[:, c % 2, :], ACT.Silu, bias=col("ln_b", c)))
                act.activation(hn_hi[:, c, :], gact[:, c % 2, :], ACT.Copy).then_inc(ln_hi, 1)

            for i in range(4):
                u = U["ev_out"] + i
                head_of(u + 2)
                act.wait_ge(unit_evac, u + 1)
                for b in range(2):
                    d = 2 * i + b
                    if d >= 2:
                        act.wait_ge(sq_added, KT * 2 + d - 1)
                    act.activation(sq[:, d % 2, :], xT[:, d, :], ACT.Square).then_inc(sq_made, 1)
            norm(2)
            ffn("f1", 1, 2, TOK)
            norm(3)
            ffn("f2", 2, 3, TOK)
            norm(4)
            mod_rows(KEY_JOB, True)
            act.wait_ge(unit_mm, U["od_gate"] + 1)
            act.activation(gact[0:16, 0, :], ps[0:16, bank(U["od_gate"]), :], ACT.Copy).then_inc(gate_rows, 1)

            head_of(U["od_gate"] + 2)
            act.wait_ge(gates_in, 1)
            link(act.activation(GATE["abs"], GATE["f"], ACT.Abs))
            link(act.activation(GATE["exp"], GATE["abs"], ACT.Exp, scale=-1.0))
            act.activation(GATE["ln"], GATE["exp"], ACT.Ln, bias=1.0).then_inc(ln1p, 1)
            for n in range(5):
                head_of(U["od_in"] + 2 + n)
            act.wait_ge(arg_made, 1)
            act.activation(GATE["val"][:, :, 0:3, :], GATE["arg"][:, :, 0:3, :], ACT.Exp)
            act.activation(GATE["mm"][:, :, 1:3, :], GATE["exp"][:, :, 1:3, :], ACT.Exp)
            act.activation(GATE["lf"][:, :, 2:4, :], GATE["ln"][:, :, 2:4, :], ACT.Exp)
            act.activation(GATE["cmax"][:, :, 2:4, :], GATE["f"][:, :, 2:4, :], ACT.Exp, scale=-1.0).then_inc(val_made, 1)
            head_of(U["od_in"] + 7)
            head_of(U["od_in"] + 8)
            for i in range(4):
                s, d = 2 + i // 2, i % 2
                act.wait_ge(hid_made, i + 1)
                for h in range(HM):
                    last = act.activation(decayed[:, s - 2, d, h, :], t_ring[:, i % 2, h * P:(h + 1) * P], ACT.Exp,
                                          bias=GATE["a"][:, d, s, h:h + 1], scale=-1.0)
                last.then_inc(dec_made, 1)
            for n in range(7, 16):
                head_of(U["od_in"] + n + 2)
                if n >= 12:
                    act.wait_ge(unit_mm, U["od_in"] + n + 1)
                    for b in range(2):
                        last = act.activation(gact[:, n % 2, b * LAT:(b + 1) * LAT],
                                              ps[:, bank(U["od_in"] + n, b), 0:LAT], ACT.Sigmoid)
                    last.then_inc(gate_made, 1)
            for h in range(HM):
                act.wait_ge(kT_mm, h + 1)
                act.activation(kT[:, 2 * h:2 * h + 2, :], ps[:, 6 + h % 2, :].rearrange("p (a b) -> p a b", a=2),
                               ACT.Copy).then_inc(kT_made, 1)
            def sum_squares(n):
                s, d, h = OUTS[n]
                i = STEP_TILE[d][s] * HM + h
                act.wait_ge(h_made, n + 1)
                place = (sq if n < 12 else t_ring)[:, n // 2 % 2, (n % 2) * DH:(n % 2 + 1) * DH]
                return act.activation(place, xT[:, i, LAT:TOK], ACT.Square, accum_out=ms_cols[:, 0, i:i + 1])

            for n in range(16):
                s, d, h = OUTS[n]
                act.wait_ge(out_mm, n + 1)
                act.activation(gact[:, n % 2, 0:DH + 1], ps[:, 4 + n % 2, 0:DH + 1], ACT.Copy,
                               scale=GATE["lf"][:, d, s, h:h + 1]).then_inc(out_scaled, 1)
                if n >= 10:
                    sum_squares(n - 2)
            sum_squares(14)
            sum_squares(15).then_inc(ss_made, 1)
            act.wait_ge(ss_made, 1)
            act.activation(ms_cols[:, 1, :], ms_cols[:, 0, :], ACT.Sqrt, bias=eps[:], scale=1.0 / DH).then_inc(hsd_made, 1)
            for h in range(HM):
                act.wait_ge(hz_made, h + 1)
                act.activation(hn_hi[:, 2 * h:2 * h + 2, 0:LAT], prod[:, h % 2, :].rearrange("p (a b) -> p a b", a=2),
                               ACT.Copy).then_inc(hz_hi, 1)
            for i in range(4):
                u = U["od_out"] + i
                head_of(u + 2)
                act.wait_ge(unit_evac, u + 1)
                for b in range(2):
                    d = 2 * i + b
                    act.wait_ge(sq_added, KT * 5 + d - 1)
                    act.activation(sq[:, d % 2, 0:LAT], xT[:, d, 0:LAT], ACT.Square).then_inc(sq_made, 1)
            norm(5)
            ffn("f3", 3, 5, LAT)
            norm(6)

        @block.vector
        def _(dve):
            linked = [0]

            def link(ins):
                linked[0] += 1
                ins.then_inc(link_v, 1)
                dve.wait_ge(link_v, linked[0])

            def rest(u0, r, n):
                dve.wait_ge(hi_made, u0 + 2 * r + 1)
                dve.tensor_tensor(w_lo[:, u0 % 2, 0:n], raw[:, u0 % 2, 0:n], w_hi[:, u0 % 2, 0:n],
                                  ALU.subtract).then_inc(lo_made, 1)

            def rest_of(u):
                if u < NU:
                    rest(u, 0, SIZE[u])

            def add_square(n, d0, r, w):
                before = KT * n + d0 + 2 * r
                dve.wait_ge(sq_made, before + 1)
                if not (isinstance(r, int) and n == 0 and d0 + 2 * r == 0):
                    dve.wait_ge(sq_added, before)
                dve.tensor_tensor(acc[:, 0:w], acc[:, 0:w], sq[:, d0 % 2, 0:w], ALU.add).then_inc(sq_added, 1)

            def residual(u0, b, r, d0, vec, w):
                for s in streams(w):
                    last = dve.scalar_tensor_tensor(
                        out=xT[:, d0 + 2 * r, tokens(s)], in0=ps[:, bank(u0, b), tokens(s)],
                        scalar=modT[:, vec, d0 + 2 * r, s:s + 1], in1=xT[:, d0 + 2 * r, tokens(s)],
                        op0=ALU.mult, op1=ALU.add)
                return last

            def norm_gain(n):
                name, at = GAIN[n]
                if n < 6:
                    dve.wait_ge(mod_made, 3 * n + 2)
                    for s in range(2):
                        last = dve.scalar_tensor_tensor(out=modT[:, 3 * n + 1, :, s], in0=modT[:, 3 * n + 1, :, s],
                                                        scalar=1.0, in1=col(name, at, KT), op0=ALU.add, op1=ALU.mult)
                    link(last)

            def norm_rstd(n):
                w = W[n]
                dve.wait_ge(sd_made, n + 1)
                link(dve.reciprocal(inv[:, 1, 0:w // P], inv[:, 0, 0:w // P]))
                dve.tensor_tensor(rstd[:, 0:w].rearrange("p (i n) -> p i n", n=P),
                                  ident.unsqueeze(1).to_broadcast([P, w // P, P]),
                                  inv[:, 1, 0:w // P].unsqueeze(2).to_broadcast([P, w // P, P]),
                                  ALU.mult).then_inc(rstd_made, 1)
                dve.memset(acc[:], 0.0).then_inc(acc_clear, 1)
                dve.wait_ge(acc_clear, n + 2)

            def norm(n):
                norm_gain(n)
                norm_rstd(n)
                norm_apply(n)

            def norm_apply(n):
                w = W[n]
                name = GAIN[n][0]
                dve.wait_ge(rstd_mm, n + 1)

                def scaled(k):
                    if k >= 2 and n < 6:
                        dve.wait_ge(hn_made, KT * n + k - 1)
                    for s in streams(w):
                        gain = modT[:, 3 * n + 1, k, s:s + 1] if n < 6 else col(name, k)
                        last = dve.scalar_tensor_tensor(out=t_ring[:, k % 2, tokens(s)], in0=xT[:, k, tokens(s)],
                                                        scalar=gain, in1=ps[:, 7, tokens(s)], op0=ALU.mult, op1=ALU.mult)
                    last.then_inc(t_made if n < 6 else y_made, 1)

                if n == 6:
                    for k in range(KT):
                        if k >= 2:
                            dve.wait_ge(y_out[k % 2], 16 * (k // 2))
                        scaled(k)
                    return
                scaled(0)
                for k in range(KT):
                    if k + 1 < KT:
                        scaled(k + 1)
                    dve.wait_ge(hn_hi_made, KT * n + k + 1)
                    for s in streams(w):
                        last = dve.scalar_tensor_tensor(out=hn_lo[:, k, tokens(s)], in0=t_ring[:, k % 2, tokens(s)],
                                                        scalar=modT[:, 3 * n, k, s:s + 1], in1=hn_hi[:, k, tokens(s)],
                                                        op0=ALU.add, op1=ALU.subtract)
                    last.then_inc(hn_made, 1)
                if n in NORM_JOB:
                    mod_vector(NORM_JOB[n])

            def mod_vector(m):
                dve.wait_ge(mod_tr, m + 1)
                bias = cols[:, COLS["mod_b"][0]:COLS["mod_b"][0] + JOBS * KT].rearrange(
                    "p (m g b) -> p m b g", m=JOBS, b=2)
                to = modT[:].rearrange("p m (g b) s -> p m b g s", b=2)
                for b in range(2):
                    for s in range(2):
                        last = dve.tensor_tensor(to[:, m, b, :, s],
                                                 ps[:, column_bank(m), 8 * b:8 * b + 8].rearrange(
                                                     "p (g s) -> p g s", s=2)[:, :, s],
                                                 bias[:, m, b, :], ALU.add)
                last.then_inc(mod_made, 1)

            def ffn(name, f, n, w):
                tile = 0
                vec = 3 * n + 2
                for part, nf in zip("AB", PARTS):
                    up, down = U[f"{name}up{part}"], U[f"{name}down{part}"]
                    job, carry = JOB_OF.get(name + part, (0, 0))
                    g0 = GBASE[name] + tile
                    a0 = ABASE[name] + tile

                    def pair(r, end):
                        has = carry and (carry == nf // 2 or not end)
                        for j in range(2):
                            if end:
                                rest_of(up + j + 2 * r + 2)
                            else:
                                rest(up + j + 2, r, UNIT)
                            dve.wait_ge(gate_made, g0 + j + 2 * r + 1)
                            if not (isinstance(r, int) and a0 + j + 2 * r == 0):
                                dve.wait_ge(a_made, a0 + j + 2 * r)
                            dve.tensor_tensor(prod[:, j, 0:w], gact[:, j, 0:w], ps[:, bank(up + j, 1), 0:w],
                                              ALU.mult).then_inc(unit_evac, 1)
                            dve.wait_ge(a_hi_made, a0 + j + 2 * r + 1)
                            dve.tensor_tensor(a_lo[:, j + 2 * r, 0:w], prod[:, j, 0:w], a_hi[:, j + 2 * r, 0:w],
                                              ALU.subtract).then_inc(a_made, 1)
                            if has and j == 1:
                                mod_vector(job + r)

                    pairs(dve, nf // 2, pair, a0 == 0)
                    if name + part in TURN_JOB:
                        mod_vector(TURN_JOB[name + part])
                    if part == "A":
                        dve.wait_ge(mod_made, vec + 1)
                        link(dve.tensor_scalar(modT[:, vec, :, :], modT[:, vec, :, :], 0.5, None, ALU.mult))
                    tile += nf

                    def down_pair(r, end):
                        for j in range(2):
                            dve.wait_ge(unit_mm, down + j + 2 * r + 1)
                            residual(down + j, 0, r, j, vec, w).then_inc(unit_evac, 1)
                            if not end:
                                rest(down + j + 2, r, nf * P)
                            if part == "B":
                                add_square(n + 1, j, r, w)
                            if end:
                                rest_of(down + j + 2 * r + 2)

                    pairs(dve, KT // 2, down_pair)

            dve.memset(eps[:], EPS)
            dve.memset(acc[:], 0.0).then_inc(acc_clear, 1)
            dve.wait_ge(par_in, 64)
            dve.wait_ge(acc_clear, 1)
            for d in range(KT):
                add_square(0, d, 0, TOK)
            mod_vector(0)
            norm_rstd(0)
            rest_of(0)
            mod_vector(1)
            norm_gain(0)
            norm_apply(0)
            rest_of(1)
            ffn("f0", 0, 0, TOK)
            norm(1)

            E = U["ev_in"]
            dve.memset(upad[:, :, :, 0:PAD], 0.0)
            dve.memset(upad[:, :, :, PAD + LAT:PADDED], 0.0).then_inc(pad_clear, 1)
            dve.wait_ge(pad_clear, 1)
            two_streams = lambda ap: ap.rearrange("p (s n) -> p s n", s=2)
            def gated_value(c, gate, b):
                u = E + c if c < 2 else E + 3 + c
                dve.wait_ge(gate_made, CONV_G + c + 1)
                dve.tensor_tensor(upad[:, c, :, PAD:PAD + LAT], two_streams(gate), two_streams(ps[:, b, :]),
                                  ALU.mult).then_inc(unit_evac, 1)

            def taps(a, b):
                for n in range(a, b):
                    c, i = 2 * (n // TAPS) + n % 2, n % TAPS // 2
                    if n % TAPS == 0:
                        dve.wait_ge(unit_evac, E + 2 if n == 0 else E + 7)
                    dst, src = two_streams(y[:, c, :]), upad[:, c, :, i:i + LAT]
                    if i == 0:
                        ins = dve.tensor_scalar(dst, src, col("conv_w", c), col("conv_b", c), ALU.mult, ALU.add)
                    else:
                        dve.wait_ge(tap_done, n - 1)
                        ins = dve.scalar_tensor_tensor(out=dst, in0=src, scalar=col("conv_w", i * CT + c), in1=dst,
                                                       op0=ALU.mult, op1=ALU.add)
                    ins.then_inc(tap_done, 1)

            for c in range(2):
                rest_of(E + c + 2)
                gated_value(c, gact[:, c % 2, :], bank(E + c))

            def turn_part(i):
                n = i // 2
                if i >= 2:
                    dve.wait_ge(roped, i - 1)
                dve.tensor_tensor(t_ring[:, i % 2, 0:LAT], ps[:, bank(E + 2 + n, i % 2), 0:LAT], cos_sin[:, 0, :],
                                  ALU.mult).then_inc(*((unit_evac, 1) if i % 2 or i == 4 else (turned_one, 1)))

            def rope(i):
                dve.wait_ge(rot_mm, i + 1)
                link(dve.tensor_tensor(sq[:, i % 2, 0:LAT], ps[:, 6 + i % 2, 0:LAT],
                                       cos_sin[:, 1, :], ALU.mult))
                dve.tensor_tensor(qk[:, i, 0:LAT], t_ring[:, i % 2, 0:LAT], sq[:, i % 2, 0:LAT],
                                  ALU.add).then_inc(roped, 1)

            dve.wait_ge(ev_in, 32)
            for n in range(3):
                if n < 2:
                    rest_of(E + 4 + n)
                taps(EARLY * n // 3, EARLY * (n + 1) // 3)
                for i in range(2 * n, min(2 * n + 2, 5)):
                    dve.wait_ge(qk_raw, i + 1)
                    turn_part(i)
                for i in range(2 * n, min(2 * n + 2, 5)):
                    rope(i)
            rest_of(E + 6)

            link(dve.tensor_scalar(att_cols[:, 4, 0:NH_ATT], col("sink", 0, NH_ATT), -1.0, None, ALU.mult))

            def largest(j):
                tt, s, h2, qt = ATT[j]
                dve.wait_ge(s_mm, j + 1)
                top = att_cols[:, 0, j:j + 1]
                if s == 0:
                    link(dve.tensor_tensor_reduce(out=gact[:, j % 2, :], in0=ps[:, 4 + j % 2, :], in1=att_mask[:, qt, :],
                                                  scale=1.0, scalar=-3e38, op0=ALU.add, op1=ALU.max, accum_out=top))
                else:
                    link(dve.reduce_max(top, ps[:, 4 + j % 2, LAT:KEYS], AX.X))
                head = tt + 4 * h2
                dve.tensor_scalar(att_cols[:, 1, j:j + 1], top, -HD ** -0.5, att_cols[:, 4, head:head + 1],
                                  ALU.mult, ALU.min).then_inc(max_made, 1)

            def denominator(j):
                dve.wait_ge(exp_made, j + 1)
                den = att_cols[:, 5, j:j + 1]
                link(dve.tensor_tensor(den, att_cols[:, 2, j:j + 1], att_cols[:, 3, j:j + 1], ALU.add))
                dve.reciprocal(den, den).then_inc(den_made, 1)

            NJ = len(ATT)
            for j in range(NJ + 4):
                if j < NJ:
                    largest(j)
                if 1 <= j < NJ + 1:
                    denominator(j - 1)
                if j >= 7 and (j - 3) % 4 == 0:
                    g = (j - 7) // 4
                    dve.wait_ge(att_hi, g + 1)
                    dve.tensor_tensor(hn_lo[:, CT + g // 2, tokens(g % 2)], ps[:, g % 2, 0:LAT],
                                      hn_hi[:, CT + g // 2, tokens(g % 2)], ALU.subtract).then_inc(mix_made, 1)
                if j in (4, 9):
                    c = 2 if j == 4 else 3
                    gated_value(c, t_ring[:, c % 2, :], 2)
                if j in (11, 13):
                    rest_of(E + 7 + (j - 11) // 2)
                taps(taps_by(j - 1) if j else EARLY, taps_by(j))

            dve.wait_ge(ln_mm, 1)
            link(dve.tensor_scalar(sd[:], ps[:, 7, :], 1.0 / (CT * P), None, ALU.mult))
            for c in range(CT):
                dve.tensor_tensor(y[:, c, :], y[:, c, :], sd[:], ALU.subtract).then_inc(ln_cent, 1)
            dve.wait_ge(ln_sd, 1)
            link(dve.reciprocal(rstd[:], sd[:]))

            def ln_scaled(c):
                dve.scalar_tensor_tensor(out=t_ring[:, c % 2, :], in0=y[:, c, :], scalar=col("ln_g", c), in1=rstd[:],
                                         op0=ALU.mult, op1=ALU.mult).then_inc(ln_t, 1)

            ln_scaled(0)
            for c in range(CT):
                if c + 1 < CT:
                    ln_scaled(c + 1)
                dve.wait_ge(ln_hi, c + 1)
                dve.tensor_tensor(hn_lo[:, c, :], gact[:, c % 2, :], hn_hi[:, c, :], ALU.subtract).then_inc(mix_made, 1)


            def mix_out(name, n, w):
                for i in range(4):
                    u = U[name] + i
                    dve.wait_ge(unit_mm, u + 1)
                    residual(u, 0, 0, 2 * i, 3 * n - 1, w)
                    residual(u, 1, 0, 2 * i + 1, 3 * n - 1, w).then_inc(unit_evac, 1)
                    if i < 3:
                        rest_of(u + 2)
                    for b in range(2):
                        add_square(n, 2 * i + b, 0, w)
                rest_of(u + 2)

            mix_out("ev_out", 2, TOK)
            norm(2)
            ffn("f1", 1, 2, TOK)
            norm(3)
            ffn("f2", 2, 3, TOK)
            norm(4)
            mod_vector(KEY_JOB)

            u = U["od_gate"]
            rest_of(u + 2)
            dve.wait_ge(gates_mm, 1)
            for d in range(2):
                for s in range(4):
                    i = STEP_TILE[d][s]
                    for kind, name in enumerate(("li", "f")):
                        a = 8 * d + HM * kind
                        last = dve.tensor_tensor(GATE[name][:, d, s, :], ps[:, bank(u), i * 16 + a:i * 16 + a + HM],
                                                 col("b_gate", a, HM), ALU.add)
            last.then_inc(unit_evac, 1)
            dve.memset(v_tok[:, :, :, DH:DH + 1], 1.0).then_inc(gates_in, 1)
            dve.wait_ge(ln1p, 1)
            dve.scalar_tensor_tensor(out=GATE["lf"], in0=GATE["f"], scalar=0.0, in1=GATE["ln"], op0=ALU.min,
                                     op1=ALU.subtract).then_inc(lf_made, 1)

            def flat(ap):
                return ap.rearrange("p d s h -> p (d s h)")

            def spread(i, values):
                if i >= 2:
                    dve.wait_ge(diag_mm, i - 1)
                dve.tensor_tensor(sq[:, i % 2, :].rearrange("p (h n) -> p h n", h=HM),
                                  ident.unsqueeze(1).to_broadcast([P, HM, P]),
                                  values.unsqueeze(2).to_broadcast([P, HM, P]), ALU.mult).then_inc(diag_made, 1)

            def diagonal(i):
                if i < 8:
                    spread(i, GATE["a"][:, i // 4, i % 4, :])
                else:
                    spread(i, GATE["mq"][:, i % 2, 2 + (i - 8) // 2, :])

            def four(ap):
                return ap.rearrange("p (h n) -> p h n", h=HM)

            def maxima(i):
                d, s = i // 4, i % 4
                dve.wait_ge(diag_mm, i + 1)
                bk = four(ps[:, 4 + i % 2, :])
                if s >= 2:
                    hide = mat["hide_after" if d == 0 else "hide_before"]
                    link(dve.tensor_tensor(four(t_ring[:, i % 2, :]), bk, hide.unsqueeze(1).to_broadcast([P, HM, P]),
                                           ALU.add))
                    dve.tensor_reduce(GATE["cmax"][:, d, s, :], four(t_ring[:, i % 2, :]), AX.X, ALU.max)
                if s < 3:
                    dve.tensor_reduce(GATE["amax"][:, d, s, :], bk, AX.X, ALU.max)

            def hidden(i):
                d = i % 2
                dve.wait_ge(diag_mm, 8 + i + 1)
                if i >= 2:
                    dve.wait_ge(dec_made, i - 1)
                hide = mat["hide_before" if d == 0 else "hide_after"]
                dve.tensor_tensor(four(t_ring[:, i % 2, :]), four(ps[:, 4 + i % 2, :]),
                                  hide.unsqueeze(1).to_broadcast([P, HM, P]), ALU.subtract).then_inc(hid_made, 1)

            def chain():
                g = GATE
                link(dve.memset(g["m"][:, :, 0, :], 0.0))
                for s in range(3):
                    link(dve.tensor_tensor(g["mm"][:, :, s, :], g["m"][:, :, s, :], g["amax"][:, :, s, :], ALU.max))
                    link(dve.tensor_tensor(g["m"][:, :, s + 1, :], g["end"][:, :, s, :], g["mm"][:, :, s, :], ALU.add))
                link(dve.tensor_tensor(g["mq"][:, :, 2:4, :], g["cmax"][:, :, 2:4, :], g["m"][:, :, 2:4, :], ALU.max))
                dve.tensor_tensor(g["arg"][:, :, 0:3, :], g["a"][:, :, 0:3, :], g["mm"][:, :, 0:3, :], ALU.subtract)
                dve.tensor_tensor(g["f"][:, :, 2:4, :], g["b"][:, :, 2:4, :], g["mq"][:, :, 2:4, :], ALU.add)
                dve.tensor_tensor(g["exp"][:, :, 0:3, :], g["m"][:, :, 0:3, :], g["mm"][:, :, 0:3, :], ALU.subtract)
                dve.tensor_tensor(g["ln"][:, :, 2:4, :], g["m"][:, :, 2:4, :], g["mq"][:, :, 2:4, :],
                                  ALU.subtract).then_inc(arg_made, 1)

            for n in range(16):
                u = U["od_in"] + n
                rest_of(u + 2)
                dve.wait_ge(unit_mm, u + 1)
                h = n % 4
                if n == 0:
                    for i in range(4):
                        last = dve.tensor_scalar(k_tok[:, i, h, :], ps[:, KEY_BANKS[i], 0:DH], DH ** -0.5, None,
                                                 ALU.mult)
                elif n < 4:
                    for b in range(2):
                        last = dve.tensor_scalar(k_tok[:, 2 * b:2 * b + 2, h, :], two_streams(ps[:, bank(u, b), :]),
                                                 DH ** -0.5, None, ALU.mult)
                elif n < 8:
                    for b in range(2):
                        last = dve.tensor_copy(v_tok[:, 2 * b:2 * b + 2, h, 0:DH], two_streams(ps[:, bank(u, b), :]))
                elif n < 12:
                    for b in range(2):
                        last = dve.tensor_copy(qT[:, 2 * h + b, :], ps[:, bank(u, b), 0:LAT])
                else:
                    dve.wait_ge(gate_made, OD_G + h + 1)
                    for b in range(2):
                        last = dve.tensor_scalar(oT[:, 2 * h + b, :], gact[:, n % 2, b * LAT:(b + 1) * LAT],
                                                 col("norm_g", 2 * h + b), None, ALU.mult)
                last.then_inc(unit_evac, 1)
                if n == 0:
                    dve.wait_ge(cum_mm, 1)
                    dve.tensor_copy(flat(GATE["b"]), ps[:, 7, 0:32])
                    dve.tensor_copy(flat(GATE["end"]), ps[:, 7, 32:64])
                    link(dve.tensor_tensor(flat(GATE["a"]), flat(GATE["li"]), ps[:, 7, 0:32], ALU.subtract))
                    diagonal(0)
                    diagonal(1)
                if 1 <= n <= 4:
                    for i in range(2 * n - 2, 2 * n):
                        maxima(i)
                        if i + 2 < 8:
                            diagonal(i + 2)
                if n == 4:
                    chain()
                    diagonal(8)
                    diagonal(9)
                if n == 5:
                    hidden(0)
                    diagonal(10)
                    hidden(1)
                    diagonal(11)
                if n == 6:
                    hidden(2)
                    hidden(3)

            for i in range(4):
                s, d = 2 + i // 2, i % 2
                dve.wait_ge(dec_made, i + 1)
                dve.wait_ge(st_mm, STEP_TILE[d][s] + 1)
                dve.tensor_tensor(decayed[:, s - 2, d], decayed[:, s - 2, d], four(ps[:, 4 + STEP_TILE[d][s], :]),
                                  ALU.mult).then_inc(sT_made, 1)
            dve.wait_ge(val_made, 1)

            def weighted(n):
                s, d, h = STATES[n]
                if n >= 2:
                    dve.wait_ge(st_up, n - 1)
                dve.tensor_scalar(t_ring[:, n % 2, 0:DH], k_tok[:, STEP_TILE[d][s], h, :],
                                  GATE["val"][:, d, s, h:h + 1], None, ALU.mult).then_inc(wk_made, 1)

            def new_state(n):
                s, d, h = STATES[n]
                dve.wait_ge(st_up, n + 1)
                for kt in range(2):
                    src = ps[:, 2 * (n % 2) + kt, 0:DH + 1]
                    if s == 0:
                        last = dve.tensor_copy(state[:, d, h, kt, :], src)
                    else:
                        last = dve.scalar_tensor_tensor(out=state[:, d, h, kt, :], in0=state[:, d, h, kt, :],
                                                        scalar=GATE["mm"][:, d, s, h:h + 1], in1=src,
                                                        op0=ALU.mult, op1=ALU.add)
                last.then_inc(st_made, 1)

            def head_output(n):
                s, d, h = OUTS[n]
                i = STEP_TILE[d][s]
                dve.wait_ge(out_scaled, n + 1)
                total = prod[:, n % 2, 0:DH + 1]
                dve.tensor_tensor(total, gact[:, n % 2, 0:DH + 1], ps[:, 6 + n % 2, 0:DH + 1],
                                  ALU.add).then_inc(out_made, 1)
                dve.wait_ge(out_made, n + 1)
                den = out_cols[:, 0, n:n + 1]
                whole = total[:, DH:DH + 1]
                link(dve.scalar_tensor_tensor(out=den, in0=whole, scalar=-1.0, in1=whole, op0=ALU.mult, op1=ALU.max))
                link(dve.tensor_tensor(den, den, GATE["cmax"][:, d, s, h:h + 1], ALU.max))
                link(dve.reciprocal(den, den))
                dst = xT[:, i * HM + h, LAT:TOK]
                if s == 2:
                    dve.tensor_scalar(dst, total[:, 0:DH], den, None, ALU.mult).then_inc(h_made, 1)
                else:
                    dve.scalar_tensor_tensor(out=dst, in0=total[:, 0:DH], scalar=den, in1=dst, op0=ALU.mult,
                                             op1=ALU.add).then_inc(h_made, 1)

            def states(a, b):
                weighted(a)
                for n in range(a, b):
                    if n + 1 < b:
                        weighted(n + 1)
                    new_state(n)

            states(0, 16)
            for n in range(8):
                head_output(n)
            states(16, 24)
            for n in range(8, 16):
                head_output(n)

            dve.wait_ge(hsd_made, 1)
            link(dve.reciprocal(ms_cols[:, 1, :], ms_cols[:, 1, :]))
            for h in range(HM):
                for i in (h, HM + h):
                    dve.tensor_scalar(xT[:, i, LAT:TOK], xT[:, i, LAT:TOK], ms_cols[:, 1, i:i + 1], None,
                                      ALU.mult).then_inc(hnorm, 1)

            def gated(h):
                dve.wait_ge(hT_mm, h + 1)
                if h >= 2:
                    dve.wait_ge(mix_made, CT + 8 + h - 1)
                dve.tensor_tensor(two_streams(prod[:, h % 2, :]), two_streams(ps[:, 6 + h % 2, :]),
                                  oT[:, 2 * h:2 * h + 2, :], ALU.mult).then_inc(hz_made, 1)

            gated(0)
            for h in range(HM):
                if h + 1 < HM:
                    gated(h + 1)
                dve.wait_ge(hz_hi, h + 1)
                dve.tensor_tensor(hn_lo[:, 2 * h:2 * h + 2, 0:LAT], two_streams(prod[:, h % 2, :]),
                                  hn_hi[:, 2 * h:2 * h + 2, 0:LAT], ALU.subtract).then_inc(mix_made, 1)
            mix_out("od_out", 5, LAT)
            norm(5)
            ffn("f3", 3, 5, LAT)
            norm(6)


def columns(a):
    return np.ascontiguousarray(a).reshape(-1, P).T


def tiles(w, width):
    k, n = w.shape
    return w.reshape(k // P, P, n // width, width).transpose(2, 1, 0, 3).reshape(n // width, P, -1)


def shape_constants():
    i = np.arange(P)
    up = (i[:, None] <= i[None, :]).astype(np.float32)
    rot = np.zeros((P, P), np.float32)
    for a in range(0, P, 2 * ROPE_FREQS):
        for j in range(ROPE_FREQS):
            rot[a + ROPE_FREQS + j, a + j] = -1.0
            rot[a + j, a + ROPE_FREQS + j] = 1.0
    mats = {
        "ident": np.eye(P, dtype=np.float32),
        "ones": np.ones((P, P), np.float32),
        "tri_up": up,
        "tri_low": np.ascontiguousarray(up.T),
        "hide_after": np.where(i[None, :] > i[:, None], np.float32(-BIG), np.float32(0)),
        "hide_before": np.where(i[None, :] < i[:, None], np.float32(-BIG), np.float32(0)),
        "rot": rot,
    }
    tok = np.arange(LAT)
    place = np.stack([tok // GRID_W, tok % GRID_W]).astype(np.float32)
    inv = np.float32(10000.0) ** (-np.arange(ROPE_FREQS, dtype=np.float32) / np.float32(ROPE_FREQS))
    feature = np.arange(P) % HD
    angle = place[feature // (2 * ROPE_FREQS)] * inv[feature % ROPE_FREQS][:, None]
    cos_sin = np.stack([np.cos(angle), np.sin(angle)], axis=1).astype(np.float32)
    query = np.arange(P)[:, None, None] + P * np.arange(2)[None, :, None]
    key = np.arange(KEYS)[None, None, :]
    hidden = (key < LAT) & (np.abs(key - query) > WINDOW)
    mask = np.where(hidden, np.float32(-BIG), np.float32(0))
    sel = np.zeros((P, 8), np.float32)
    for g in range(4):
        for s in range(2):
            sel[32 * g + s, 2 * g + s] = 1.0
    return {"mats": np.stack([mats[n] for n in MATS], axis=1), "cos_sin": cos_sin, "att_mask": mask, "sel": sel}


def layout(x, c, ctx, c_ctx, mod_w, mod_b, ffn1_norm, ffn1_w_gu, ffn1_w_d, mix_norm, ffn2_norm, ffn2_w_gu,
           ffn2_w_d, ev_w_in, ev_conv_w, ev_conv_b, ev_conv_ln_g, ev_conv_ln_b, ev_sink, ev_w_out, od_w_in,
           od_b_gate, od_norm_g, od_w_out, final_norm):
    put = shape_constants()
    put["xT"] = np.concatenate([x[0], ctx[0]], axis=0).T.reshape(KT, P, TOK).transpose(1, 0, 2)
    cond = np.zeros((P, KT, 32), np.float32)
    cond[:, :, 0] = columns(c)
    cond[:, :, 1] = columns(c_ctx)
    put["c_in"] = cond.reshape(P, KT * 32)
    put["cols"] = np.concatenate(
        [columns(ffn1_norm), columns(mix_norm), columns(ffn2_norm), columns(final_norm), columns(ev_conv_b),
         columns(ev_conv_ln_g), columns(ev_conv_ln_b), columns(od_norm_g), columns(ev_conv_w), columns(mod_b),
         np.broadcast_to(ev_sink.reshape(1, -1), (P, NH_ATT)), np.broadcast_to(od_b_gate.reshape(1, -1), (P, 4 * HM))],
        axis=1)
    put["mod_w"] = mod_w.reshape(2, KT, P, NVEC, D).transpose(0, 3, 2, 1, 4).reshape(JOBS, P, KT, D)
    ups = [ffn1_w_gu[0], ffn2_w_gu[0], ffn1_w_gu[1], ffn2_w_gu[1]]
    downs = [ffn1_w_d[0], ffn2_w_d[0], ffn1_w_d[1], ffn2_w_d[1]]
    put["w_up"] = np.stack([w.reshape(KT, P, 2, FT, P).transpose(3, 1, 2, 0, 4).reshape(FT, P, UNIT) for w in ups])
    cut = PARTS[0] * P
    put["w_downA"] = np.stack([tiles(w[:cut], P) for w in downs])
    put["w_downB"] = np.stack([tiles(w[cut:], P) for w in downs])
    w = ev_w_in[0]
    half = CT * P
    conv = [np.concatenate([tiles(w[:, P * i:P * (i + 1)], P)[0], tiles(w[:, half + P * i:half + P * (i + 1)], P)[0]],
                           axis=1) for i in range(CT)]
    q_off = 2 * half
    query = [np.concatenate([w[:, q_off + HD * h:q_off + HD * (h + 1)] for h in (i, i + 4)], axis=1) for i in range(4)]
    kv = [w[:, q_off + half + P * i:q_off + half + P * (i + 1)] for i in range(2)]
    pairs = [(query[0], query[1]), (query[2], query[3]), (kv[0], kv[1])]
    mixed = [np.concatenate([tiles(m, P)[0] for m in p], axis=1) for p in pairs]
    put["w_ev_in"] = np.stack(conv[:2] + mixed + conv[2:])
    w = ev_w_out[0]
    rows = [w[:half]] + [w[half + HD * h:half + HD * (h + 1)] for i in range(4) for h in (i, i + 4)]
    w = np.concatenate(rows, axis=0)

    def two_wide(w):
        k, n = w.shape
        return w.reshape(k // P, P, n // (2 * P), 2, P).transpose(2, 1, 3, 0, 4).reshape(n // (2 * P), P, -1)

    put["w_ev_out"] = two_wide(w)
    w = od_w_in[0]
    put["w_od_in"] = np.concatenate([tiles(w[:, D * i:D * (i + 1)], DH) for i in (1, 2, 0, 3)], axis=0)
    put["w_od_gate"] = tiles(w[:, 4 * D:], 4 * HM)[0]
    put["w_od_out"] = two_wide(od_w_out[0])
    return {n: np.ascontiguousarray(a) for n, a in put.items()}


def kernel(**inputs):
    import concourse.bacc as bacc
    from concourse.bass_utils import run_bass_kernel_spmd

    nc = bacc.Bacc("TRN2", target_bir_lowering=False, num_devices=1)
    arrays = layout(**{n: np.asarray(a) for n, a in inputs.items()})
    t = {n: nc.dram_tensor(f"in_{n}", a.shape, mybir.dt.from_np(a.dtype), kind="ExternalInput").ap()
         for n, a in arrays.items()}
    out = nc.dram_tensor("out_y", (P, KT, LAT), F32, kind="ExternalOutput").ap()
    build(nc, t, out)
    r = run_bass_kernel_spmd(nc, [{f"in_{n}": a for n, a in arrays.items()}], core_ids=[0])
    y = r.results[0]["out_y"]
    return y.transpose(2, 1, 0).reshape(1, LAT, D)
```
